# Optimizing a Trainium2 kernel written in Bass

```python
import math
import jax, jax.numpy as jnp
from jax import lax
import numpy as np

D_MODEL = 2048
BATCH = 1
SEQ = 256
DEPTH = 1

N_MIXERS = 3
EPS = 1e-6
PLE_DIM = 256
D_FF = -(-8 * D_MODEL // (3 * 256)) * 256

SB_HEAD_DIM = 128
SB_HEADS = D_MODEL // SB_HEAD_DIM
Q_BLOCK = 128

S5_GROUP = 16
S5_GROUPS = D_MODEL // S5_GROUP
S5_STATE = 64
S5_CHUNK = 128

ML_HEADS = 8
ML_QK_DIM = D_MODEL // ML_HEADS // 2
ML_V_DIM = D_MODEL // ML_HEADS
ML_NQK = ML_HEADS * ML_QK_DIM
ML_IN = 2 * ML_NQK + 2 * D_MODEL + 2 * ML_HEADS
ML_CHUNK = 128

N_SB = (DEPTH + 2) // N_MIXERS
N_S5 = (DEPTH + 1) // N_MIXERS
N_ML = DEPTH // N_MIXERS

kernel_name = "hybrid_sb_s5_mlstm_trunk"

def rms_norm(x, g):
    xf = x.astype(jnp.float32)
    y = xf * lax.rsqrt(jnp.mean(xf * xf, axis=-1, keepdims=True) + EPS)
    return (y * g.astype(jnp.float32)).astype(x.dtype)

def split_heads(t, n, d):
    b, l, _ = t.shape
    return t.reshape(b, l, n, d).transpose(0, 2, 1, 3)

def stick_breaking_attention(h, w_in, q_gain, k_gain, w_out):
    bsz, seq, _ = h.shape
    q, k, v = jnp.split(h @ w_in, 3, axis=-1)
    q = rms_norm(split_heads(q, SB_HEADS, SB_HEAD_DIM), q_gain).astype(jnp.float32)
    k = rms_norm(split_heads(k, SB_HEADS, SB_HEAD_DIM), k_gain).astype(jnp.float32)
    v = split_heads(v, SB_HEADS, SB_HEAD_DIM).astype(jnp.float32)
    q = q * (SB_HEAD_DIM ** -0.5)
    nb = seq // Q_BLOCK
    q_blocks = q.reshape(bsz, SB_HEADS, nb, Q_BLOCK, SB_HEAD_DIM).transpose(2, 0, 1, 3, 4)
    key_pos = jnp.arange(seq)

    def block(args):
        qb, b = args
        z = jnp.einsum('bhqd,bhkd->bhqk', qb, k)
        q_pos = b * Q_BLOCK + jnp.arange(Q_BLOCK)
        strict = key_pos[None, :] < q_pos[:, None]
        log_1m = jnp.where(strict, jax.nn.log_sigmoid(-z), 0.0)
        rest = lax.cumsum(log_1m, axis=3, reverse=True) - log_1m
        a = jnp.where(strict, jnp.exp(jax.nn.log_sigmoid(z) + rest), 0.0)
        return jnp.einsum('bhqk,bhkd->bhqd', a, v)

    o = lax.map(block, (q_blocks, jnp.arange(nb)))
    o = o.transpose(1, 0, 3, 2, 4).reshape(bsz, seq, D_MODEL).astype(h.dtype)
    return o @ w_out

def s5_layer(h, w_in, lam_re, lam_im, log_dt, b_re, b_im, c_re, c_im, d_skip, w_glu, w_out):
    bsz, seq, _ = h.shape
    f32 = jnp.float32
    u = (h @ w_in).astype(f32).reshape(bsz, seq, S5_GROUPS, S5_GROUP)
    dt = jnp.exp(log_dt.astype(f32))[:, None]
    lr, li = lam_re.astype(f32), lam_im.astype(f32)
    mag = jnp.exp(lr * dt)
    ar, ai = mag * jnp.cos(li * dt), mag * jnp.sin(li * dt)
    den = lr * lr + li * li
    cr = ((ar - 1.0) * lr + ai * li) / den
    ci = (ai * lr - (ar - 1.0) * li) / den
    br, bi = b_re.astype(f32), b_im.astype(f32)
    bbr = cr[..., None] * br - ci[..., None] * bi
    bbi = cr[..., None] * bi + ci[..., None] * br
    cre, cim, dsk = c_re.astype(f32), c_im.astype(f32), d_skip.astype(f32)

    nc = seq // S5_CHUNK
    u_c = u.reshape(bsz, nc, S5_CHUNK, S5_GROUPS, S5_GROUP).transpose(1, 2, 0, 3, 4)
    a_r = jnp.broadcast_to(ar, (S5_CHUNK, bsz, S5_GROUPS, S5_STATE))
    a_i = jnp.broadcast_to(ai, (S5_CHUNK, bsz, S5_GROUPS, S5_STATE))

    def combine(e1, e2):
        a1r, a1i, x1r, x1i = e1
        a2r, a2i, x2r, x2i = e2
        return (a2r * a1r - a2i * a1i, a2r * a1i + a2i * a1r,
                a2r * x1r - a2i * x1i + x2r, a2r * x1i + a2i * x1r + x2i)

    def chunk_step(carry, uc):
        sr, si = carry
        bur = jnp.einsum('gpc,tbgc->tbgp', bbr, uc)
        bui = jnp.einsum('gpc,tbgc->tbgp', bbi, uc)
        pr, pi, xr, xi = lax.associative_scan(combine, (a_r, a_i, bur, bui), axis=0)
        xr = xr + pr * sr - pi * si
        xi = xi + pr * si + pi * sr
        y = (jnp.einsum('gcp,tbgp->tbgc', cre, xr) - jnp.einsum('gcp,tbgp->tbgc', cim, xi)
             + dsk * uc)
        return (xr[-1], xi[-1]), y

    init = (jnp.zeros((bsz, S5_GROUPS, S5_STATE), f32), jnp.zeros((bsz, S5_GROUPS, S5_STATE), f32))
    _, y = lax.scan(chunk_step, init, u_c)
    y = y.transpose(2, 0, 1, 3, 4).reshape(bsz, seq, D_MODEL).astype(h.dtype)
    g = jax.nn.gelu(y)
    g = g * jax.nn.sigmoid(g @ w_glu)
    return g @ w_out

def mlstm_layer(h, w_in, gate_bias, head_gain, w_out):
    bsz, seq, _ = h.shape
    f32 = jnp.float32
    proj = h @ w_in
    q, k, v, o, gi = jnp.split(proj, [ML_NQK, 2 * ML_NQK, 2 * ML_NQK + D_MODEL, 2 * ML_NQK + 2 * D_MODEL], axis=-1)
    q = split_heads(q, ML_HEADS, ML_QK_DIM).astype(f32)
    k = split_heads(k, ML_HEADS, ML_QK_DIM).astype(f32) * (ML_QK_DIM ** -0.5)
    v = split_heads(v, ML_HEADS, ML_V_DIM).astype(f32)
    gates = gi.astype(f32) + gate_bias.astype(f32)
    i_pre = gates[..., :ML_HEADS].transpose(0, 2, 1)
    log_f = jax.nn.log_sigmoid(gates[..., ML_HEADS:]).transpose(0, 2, 1)
    nc = seq // ML_CHUNK

    def to_chunks(t):
        t = t.reshape(bsz, ML_HEADS, nc, ML_CHUNK, *t.shape[3:])
        return jnp.moveaxis(t, 2, 0)

    causal = jnp.tril(jnp.ones((ML_CHUNK, ML_CHUNK), dtype=bool))

    def step(carry, xs):
        c_st, n_st, m_st = carry
        qc, kc, vc, ic, fc = xs
        bcum = jnp.cumsum(fc, axis=-1)
        dmat = jnp.where(causal, bcum[..., :, None] - bcum[..., None, :] + ic[..., None, :], -jnp.inf)
        inter = bcum + m_st[..., None]
        m_row = jnp.maximum(jnp.max(dmat, axis=-1), inter)
        w = jnp.exp(dmat - m_row[..., None])
        w_inter = jnp.exp(inter - m_row)
        s = jnp.einsum('bhtd,bhsd->bhts', qc, kc) * w
        num = (jnp.einsum('bhts,bhsv->bhtv', s, vc)
               + w_inter[..., None] * jnp.einsum('bhtd,bhdv->bhtv', qc, c_st))
        den = jnp.sum(s, axis=-1) + w_inter * jnp.einsum('bhtd,bhd->bht', qc, n_st)
        h_t = num / jnp.maximum(jnp.abs(den), jnp.exp(-m_row))[..., None]
        b_last = bcum[..., -1]
        dec = b_last[..., None] - bcum + ic
        m_new = jnp.maximum(b_last + m_st, jnp.max(dec, axis=-1))
        wk = jnp.exp(dec - m_new[..., None])
        carry_scale = jnp.exp(b_last + m_st - m_new)
        c_new = carry_scale[..., None, None] * c_st + jnp.einsum('bhsd,bhsv->bhdv', kc * wk[..., None], vc)
        n_new = carry_scale[..., None] * n_st + jnp.einsum('bhs,bhsd->bhd', wk, kc)
        return (c_new, n_new, m_new), h_t

    init = (jnp.zeros((bsz, ML_HEADS, ML_QK_DIM, ML_V_DIM), f32),
            jnp.zeros((bsz, ML_HEADS, ML_QK_DIM), f32),
            jnp.zeros((bsz, ML_HEADS), f32))
    _, hs = lax.scan(step, init, (to_chunks(q), to_chunks(k), to_chunks(v), to_chunks(i_pre), to_chunks(log_f)))
    hs = jnp.moveaxis(hs, 0, 2).reshape(bsz, ML_HEADS, seq, ML_V_DIM).transpose(0, 2, 1, 3)
    hs = rms_norm(hs, head_gain).reshape(bsz, seq, D_MODEL).astype(h.dtype)
    hs = jax.nn.sigmoid(o) * hs
    return hs @ w_out

def swiglu(h, w_gate, w_up, w_down):
    return (jax.nn.silu(h @ w_gate) * (h @ w_up)) @ w_down

def setup_inputs(seed: int = 0) -> dict:
    key = jax.random.key(seed)
    ks = iter(jax.random.split(key, 40))

    def nrm(shape, scale):
        return jax.random.normal(next(ks), shape, jnp.float32) * scale

    D = D_MODEL
    G, P, GS = S5_GROUPS, S5_STATE, S5_GROUP
    n_idx = jnp.arange(P, dtype=jnp.float32)
    f_bias = jnp.linspace(3.0, 6.0, ML_HEADS, dtype=jnp.float32)
    return {
        "x": nrm((BATCH, SEQ, D), 1.0),
        "p": nrm((DEPTH, BATCH, SEQ, PLE_DIM), 1.0),
        "norm_mix": 1.0 + nrm((DEPTH, D), 0.02),
        "norm_ffn": 1.0 + nrm((DEPTH, D), 0.02),
        "sb_w_in": nrm((N_SB, D, 3 * D), D ** -0.5),
        "sb_q_gain": 1.0 + nrm((N_SB, SB_HEAD_DIM), 0.02),
        "sb_k_gain": 1.0 + nrm((N_SB, SB_HEAD_DIM), 0.02),
        "sb_w_out": nrm((N_SB, D, D), D ** -0.5),
        "s5_w_in": nrm((N_S5, D, D), D ** -0.5),
        "s5_lam_re": -0.5 * jnp.exp(nrm((N_S5, G, P), 0.05)),
        "s5_lam_im": math.pi * n_idx + nrm((N_S5, G, P), 0.05),
        "s5_log_dt": jax.random.uniform(next(ks), (N_S5, G), jnp.float32, math.log(1e-3), math.log(1e-1)),
        "s5_b_re": nrm((N_S5, G, P, GS), (2 * GS) ** -0.5),
        "s5_b_im": nrm((N_S5, G, P, GS), (2 * GS) ** -0.5),
        "s5_c_re": nrm((N_S5, G, GS, P), (2 * P) ** -0.5),
        "s5_c_im": nrm((N_S5, G, GS, P), (2 * P) ** -0.5),
        "s5_d": nrm((N_S5, G, GS), 1.0),
        "s5_w_glu": nrm((N_S5, D, D), D ** -0.5),
        "s5_w_out": nrm((N_S5, D, D), D ** -0.5),
        "ml_w_in": nrm((N_ML, D, ML_IN), D ** -0.5),
        "ml_gate_bias": jnp.concatenate([jnp.zeros((ML_HEADS,), jnp.float32), f_bias])[None, :] + nrm((N_ML, 2 * ML_HEADS), 0.1),
        "ml_head_gain": 1.0 + nrm((N_ML, ML_HEADS, ML_V_DIM), 0.02),
        "ml_w_out": nrm((N_ML, D, D), D ** -0.5),
        "ffn_w_gate": nrm((DEPTH, D, D_FF), D ** -0.5),
        "ffn_w_up": nrm((DEPTH, D, D_FF), D ** -0.5),
        "ffn_w_down": nrm((DEPTH, D_FF, D), D_FF ** -0.5),
        "ple_norm": 1.0 + nrm((DEPTH, D), 0.02),
        "ple_w_gate": nrm((DEPTH, D, D), D ** -0.5),
        "ple_w_proj": nrm((DEPTH, PLE_DIM, D), PLE_DIM ** -0.5),
    }

def reference(x, p, norm_mix, norm_ffn, sb_w_in, sb_q_gain, sb_k_gain, sb_w_out,
              s5_w_in, s5_lam_re, s5_lam_im, s5_log_dt, s5_b_re, s5_b_im, s5_c_re, s5_c_im,
              s5_d, s5_w_glu, s5_w_out, ml_w_in, ml_gate_bias, ml_head_gain, ml_w_out,
              ffn_w_gate, ffn_w_up, ffn_w_down, ple_norm, ple_w_gate, ple_w_proj):
    for i in range(DEPTH):
        kind, j = i % N_MIXERS, i // N_MIXERS
        hn = rms_norm(x, norm_mix[i])
        if kind == 0:
            y = stick_breaking_attention(hn, sb_w_in[j], sb_q_gain[j], sb_k_gain[j], sb_w_out[j])
        elif kind == 1:
            y = s5_layer(hn, s5_w_in[j], s5_lam_re[j], s5_lam_im[j], s5_log_dt[j], s5_b_re[j], s5_b_im[j],
                         s5_c_re[j], s5_c_im[j], s5_d[j], s5_w_glu[j], s5_w_out[j])
        else:
            y = mlstm_layer(hn, ml_w_in[j], ml_gate_bias[j], ml_head_gain[j], ml_w_out[j])
        x = x + y
        x = x + swiglu(rms_norm(x, norm_ffn[i]), ffn_w_gate[i], ffn_w_up[i], ffn_w_down[i])
        gate = jax.nn.sigmoid(rms_norm(x, ple_norm[i]) @ ple_w_gate[i])
        x = x + gate * (p[i] @ ple_w_proj[i])
    return x


_drawn_inputs = setup_inputs


def setup_inputs(seed=0):
    import zlib

    import numpy as np

    out = dict(_drawn_inputs(seed))
    spreads = {}
    factors = {'norm_mix': 4.145, 'norm_ffn': 4.869, 'sb_q_gain': 8.0, 'sb_k_gain': 8.0, 'ple_norm': 8.0}
    for name, (base, spread) in spreads.items():
        noise = np.random.default_rng([zlib.crc32(name.encode()), seed]).standard_normal(out[name].shape)
        drawn = base * np.exp(spread * noise) if base else spread * noise
        out[name] = __import__('jax').numpy.asarray(drawn.astype(out[name].dtype))
    for name, factor in factors.items():
        out[name] = (out[name] * factor).astype(out[name].dtype)
    return out
```

```python
from contextlib import ExitStack

import numpy as np
import concourse.bass as bass
from concourse import mybir

F32 = mybir.dt.float32
F32R = mybir.dt.float32r
ACT = mybir.ActivationFunctionType
ALU = mybir.AluOpType
AX_X = mybir.AxisListType.X

P = 128
NT = 512
RING = 4
EPS = 1e-6
MASKED = -1e30


def trunk(nc, x_in, p_in, g_mix, g_ffn, w_in, g_q, g_k, w_o, w_gate, w_up, w_down, g_ple, w_pg, w_pp, out):
    _, SEQ, D = x_in.shape
    TB = SEQ // P
    KD = D // P
    FF = w_gate.shape[1]
    KF = FF // P
    KP = w_pp.shape[0] // P
    HD = g_q.shape[1]
    HEADS = D // HD
    HG = NT // HD
    GROUPS = HEADS // HG
    XN = D // NT
    FN = FF // NT
    CB = NT // P
    assert TB == 2 and HD == P and D % NT == 0 and FF % NT == 0 and KP == 2 and KD == 16 and HG == 4

    D_UNITS = [[2 * i, 2 * i + 1] for i in range(KD // 2)]
    F_UNITS = [[2 * i, 2 * i + 1] for i in range(KF // 2 - 2)] + [[c] for c in range(KF - 4, KF)]
    G_UNITS = [[2 * i, 2 * i + 1] for i in range(5)] + [[c] for c in range(10, KD)]
    DU, FU, EU = len(D_UNITS), len(F_UNITS), len(G_UNITS) + 1
    AU = 3 * DU
    CU = 2 * DU
    B_HEAD = [(t, D_UNITS[u]) for t in range(2) for u in range(6)] + [(t, D_UNITS[u]) for t in range(2) for u in (6, 7)]
    BH = len(B_HEAD)
    B_END = [B_HEAD.index((t, D_UNITS[7])) for t in range(2)]
    assert all(n % RING == 0 for n in (AU, CU, FU, EU, BH, DU))
    A0 = 0
    B0 = A0 + GROUPS * AU
    B2 = B0 + BH
    C0 = B2 + (XN - 2) * DU
    D0 = C0 + FN * CU
    E0 = D0 + XN * FU
    TA, TBO = 0, 3 * GROUPS
    TC = TBO + XN
    TD = TC + 2 * FN
    TE = TD + XN
    A_P0, A_P1 = 0, 0
    B_P0, B_P1 = 2 * GROUPS, GROUPS
    C_P0, C_P1 = B_P0 + XN - 1, B_P1 + 1
    D_P0 = C_P0 + FN
    E_P0, E_P1 = D_P0 + XN, C_P1 + FN
    X_ROUNDS = KD // 2 + 1
    B_LEFT = [(0, B_P0 + 1), (1, B_P1 + 1), (0, B_P0 + 2), (0, B_P0 + 3)]
    SETS0 = X_ROUNDS + 4 * GROUPS
    SETS0_T0, SETS0_T1 = (X_ROUNDS + 1) // 2 + 4 * GROUPS, X_ROUNDS // 2
    C_SET, D_SET, E_SET = XN - 1, XN - 1 + FN, XN - 1 + FN + XN

    with ExitStack() as ctx:
        def sb(name, shape, dt=F32, where=ctx):
            return where.enter_context(nc.sbuf_tensor(name, shape, dt))

        def sem(name):
            return ctx.enter_context(nc.semaphore(name))

        x = sb("x", [P, TB, D])
        xT = [sb("xT_hi", [P, KD, SEQ], F32R), sb("xT_lo", [P, KD, SEQ], F32R)]
        pT = [sb("pT_hi", [P, KP, SEQ], F32R), sb("pT_lo", [P, KP, SEQ], F32R)]
        raw = sb("raw", [P, RING, 2, NT])
        w_parts = [sb("w_hi", [P, RING, 2, NT], F32R), sb("w_lo", [P, RING, 2, NT], F32R)]
        stage = sb("stage", [P, TB, NT])
        junk = sb("junk", [P, NT])
        ident = sb("ident", [P, P])
        gains = sb("gains", [P, 3 * KD + 2])
        MIX, FFN, PLE, QG, KG = 0, KD, 2 * KD, 3 * KD, 3 * KD + 1
        x_ssq = sb("x_ssq", [P, XN, TB])
        pair_sum = sb("pair_sum", [P, 2, TB])
        mean_sq = sb("mean_sq", [P, TB])
        newton = sb("newton", [P, TB * HG])
        rstd = sb("rstd", [P, TB])
        rstd2 = sb("rstd2", [P, TB])
        head_ssq = sb("head_ssq", [P, TB * HG])
        head_ms = sb("head_ms", [P, TB * HG])
        head_r = sb("head_r", [P, TB * HG])
        head_scale = sb("head_scale", [P, TB * HG])
        minus_half = sb("minus_half", [P, TB * HG])
        with ExitStack() as attention:
            def at(name, shape, dt=F32):
                return sb(name, shape, dt, attention)
            oT = [at("oT_hi", [P, HEADS, SEQ], F32R), at("oT_lo", [P, HEADS, SEQ], F32R)]
            squares = at("squares", [P, TB, NT])
            normed = at("normed", [P, TB, NT])
            qT = at("qT", [P, HG, SEQ])
            kT = at("kT", [P, HG, SEQ])
            v = at("v", [P, TB, NT])
            softplus = at("softplus", [P, 3 * P])
            neg_log_1m = at("neg_log_1m", [P, 3 * P])
            weight = [at(f"weight{i}", [P, 3 * P]) for i in range(2)]
            later = at("later", [P, P])
            ones = at("ones", [P, P])
            seen = at("seen", [P, 2, P])
            unseen = at("unseen", [P, 2, P])
            gain_rows = at("gain_rows", [3 * KD + 2, P])
            p_sb = at("p_sb", [P, TB, KP * P])
        hT = [sb("hT_hi", [P, KF, SEQ], F32R), sb("hT_lo", [P, KF, SEQ], F32R)]

        acc = [[ctx.enter_context(nc.psum_tensor(f"acc{i}{tb}", [P, NT], F32)) for tb in range(TB)] for i in range(2)]
        Z = ctx.enter_context(nc.psum_tensor("Z", [P, NT], F32))
        R = ctx.enter_context(nc.psum_tensor("R", [P, NT], F32))
        T = [ctx.enter_context(nc.psum_tensor(f"T{i}", [P, 2, SEQ], F32)) for i in range(2)]
        O = T[1]

        landed = [sem(f"landed{s}") for s in range(RING)]
        hi_ready = sem("hi_ready")
        lo_ready = sem("lo_ready")
        unit_used = sem("unit_used")
        half_done = sem("half_done")
        acc_free = [[sem(f"acc_free{i}{tb}") for tb in range(TB)] for i in range(2)]
        x_loaded = [sem(f"x_loaded{j}") for j in range(XN)]
        p_loaded = sem("p_loaded")
        gains_loaded = sem("gains_loaded")
        zeroed = sem("zeroed")
        consts_ready = sem("consts_ready")
        gains_turned = sem("gains_turned")
        gains_ready = sem("gains_ready")
        T_ready = sem("T_ready")
        T_free = [sem("T_free0"), sem("T_free1")]
        turned_hi = sem("turned_hi")
        x_ssq_ready = sem("x_ssq_ready")
        rstd_ready = sem("rstd_ready")
        pool_step = sem("pool_step")
        squares_ready = sem("squares_ready")
        head_ssq_ready = sem("head_ssq_ready")
        head_scale_ready = sem("head_scale_ready")
        z_ready = sem("z_ready")
        act_step = sem("act_step")
        softplus_ready = sem("softplus_ready")
        dve_step = sem("dve_step")
        z_free = sem("z_free")
        log_1m_ready = sem("log_1m_ready")
        log_sig_ready = sem("log_sig_ready")
        rest_ready = sem("rest_ready")
        exponent_ready = sem("exponent_ready")
        weight_ready = sem("weight_ready")
        o_ready = sem("o_ready")
        oT_hi_ready = sem("oT_hi_ready")
        oT_ready = sem("oT_ready")
        x_stored = sem("x_stored")
        sig_ready = sem("sig_ready")
        x_final = sem("x_final")
        out_done = sem("out_done")

        def left(eng, pair, tiles):
            for tb in range(TB):
                eng.wait_ge(acc_free[pair][tb], tiles)

        def rounds_of_set(k):
            return SETS0_T0 + k + 1, SETS0_T1 + k + 1

        def slot(u):
            return u % RING

        def diagonals(buffer):
            return buffer[:, :].rearrange("p (b q) -> p b q", b=3)[:, 0:3:2, :]

        block = ctx.enter_context(nc.Block())

        @block.sync
        def _(sp):
            def load(U, u, blocks, columns):
                n = len(blocks)
                if not isinstance(U, int) or U >= RING:
                    sp.wait_ge(lo_ready, U - RING + 1)
                src = columns[blocks[0] * P:(blocks[0] + n) * P, :].rearrange("(k p) n -> p k n", p=P)
                sp.dma_start(raw[:, slot(u), 0:n, :], src).then_inc(landed[slot(u)], 16)

            def group(g):
                for part in range(3):
                    columns = w_in[:, part * D:(part + 1) * D][:, bass.ts(g, NT)]
                    for u in range(DU):
                        load(A0 + g * AU + part * DU + u, part * DU + u, D_UNITS[u], columns)

            group(0)
            with sp.Fori(1, GROUPS) as g:
                group(g)
            for u, (t, blocks) in enumerate(B_HEAD):
                load(B0 + u, u, blocks, w_o[:, t * NT:(t + 1) * NT])
            with sp.Fori(0, XN - 2) as n:
                for u in range(DU):
                    load(B2 + n * DU + u, u, D_UNITS[u], w_o[:, 2 * NT:][:, bass.ts(n, NT)])
            with sp.Fori(0, FN) as j:
                for part, w in enumerate((w_gate, w_up)):
                    for u in range(DU):
                        load(C0 + j * CU + part * DU + u, u, D_UNITS[u], w[:, bass.ts(j, NT)])
            with sp.Fori(0, XN) as n:
                for u in range(FU):
                    load(D0 + n * FU + u, u, F_UNITS[u], w_down[:, bass.ts(n, NT)])
            with sp.Fori(0, XN) as n:
                for u, blocks in enumerate(G_UNITS):
                    load(E0 + n * EU + u, u, blocks, w_pg[:, bass.ts(n, NT)])
                load(E0 + n * EU + EU - 1, EU - 1, list(range(KP)), w_pp[:, bass.ts(n, NT)])

        @block.gpsimd
        def _(pool):
            HALF_MS = TB * HG
            pool.memset(ident[:, :], 0.0).then_inc(zeroed, 1)
            pool.memset(later[:, :], 1.0).then_inc(zeroed, 1)
            pool.memset(seen[:, :, :], 1.0).then_inc(zeroed, 1)
            pool.memset(unseen[:, :, :], 0.0).then_inc(zeroed, 1)
            pool.memset(ones[:, :], 1.0).then_inc(zeroed, 1)
            pool.memset(minus_half[:, :], -0.5).then_inc(zeroed, 1)
            pool.wait_ge(zeroed, 6)
            pool.affine_select(out=ident[:, :], in_=ident[:, :], compare_op=ALU.not_equal, fill=1.0,
                               base=0, pattern=[[-1, P]], channel_multiplier=1).then_inc(consts_ready, 1)
            pool.affine_select(out=later[:, :], in_=later[:, :], compare_op=ALU.is_gt, fill=0.0,
                               base=0, pattern=[[-1, P]], channel_multiplier=1).then_inc(consts_ready, 1)
            pool.affine_select(out=seen[:, :, :], in_=seen[:, :, :], compare_op=ALU.is_gt, fill=0.0,
                               base=0, pattern=[[0, 2], [1, P]], channel_multiplier=-1).then_inc(consts_ready, 1)
            pool.affine_select(out=unseen[:, :, :], in_=unseen[:, :, :], compare_op=ALU.is_gt, fill=MASKED,
                               base=0, pattern=[[0, 2], [1, P]], channel_multiplier=-1).then_inc(consts_ready, 1)

            def inverse_root(r, ms, n, step):
                t = newton[:, 0:n]
                pool.wait_ge(pool_step, step)
                pool.tensor_tensor(r, ms, minus_half[:, 0:n], ALU.pow).then_inc(pool_step, 1)
                pool.wait_ge(pool_step, step + 1)
                pool.tensor_tensor(t, r, r, ALU.mult).then_inc(pool_step, 1)
                pool.wait_ge(pool_step, step + 2)
                pool.tensor_tensor(t, t, ms, ALU.mult).then_inc(pool_step, 1)
                pool.wait_ge(pool_step, step + 3)
                pool.tensor_scalar(t, t, -0.5, 1.5, ALU.mult, ALU.add).then_inc(pool_step, 1)
                pool.wait_ge(pool_step, step + 4)
                pool.tensor_tensor(r, r, t, ALU.mult).then_inc(pool_step, 1)

            NORM_STEPS = 8
            HEAD_STEPS = 9

            def norm(which, step):
                pool.wait_ge(x_ssq_ready, XN * TB * (which + 1))
                pool.tensor_tensor(pair_sum[:, :, :], x_ssq[:, 0:2, :], x_ssq[:, 2:4, :], ALU.add).then_inc(pool_step, 1)
                pool.wait_ge(pool_step, step + 1)
                pool.tensor_tensor(mean_sq[:, :], pair_sum[:, 0, :], pair_sum[:, 1, :], ALU.add).then_inc(pool_step, 1)
                pool.wait_ge(pool_step, step + 2)
                pool.tensor_scalar(mean_sq[:, :], mean_sq[:, :], 1.0 / D, EPS, ALU.mult, ALU.add).then_inc(pool_step, 1)
                inverse_root(rstd[:, :], mean_sq[:, :], TB, step + 3)
                pool.wait_ge(pool_step, step + 8)
                pool.tensor_tensor(rstd2[:, :], rstd[:, :], rstd[:, :], ALU.mult).then_inc(rstd_ready, 1)

            def head_norm(n, scale, step, pair_before, tiles_before):
                pool.wait_ge(head_ssq_ready, n + 1)
                pool.wait_ge(rstd_ready, 1)
                for tb in range(TB):
                    part = slice(tb * HG, (tb + 1) * HG)
                    pool.tensor_scalar(head_ms[:, part], head_ssq[:, part], rstd2[:, tb:tb + 1], 1.0 / HD,
                                       ALU.mult, ALU.mult).then_inc(pool_step, 1)
                pool.wait_ge(pool_step, step + 2)
                pool.tensor_scalar(head_ms[:, :], head_ms[:, :], EPS, 1.0, ALU.add, ALU.mult).then_inc(pool_step, 1)
                inverse_root(head_r[:, :], head_ms[:, :], HALF_MS, step + 3)
                pool.wait_ge(pool_step, step + 8)
                left(pool, pair_before, tiles_before)
                for tb in range(TB):
                    part = slice(tb * HG, (tb + 1) * HG)
                    last = pool.tensor_scalar(head_scale[:, part], head_r[:, part], rstd[:, tb:tb + 1], scale,
                                              ALU.mult, ALU.mult)
                    last.then_inc(pool_step if tb == 0 else head_scale_ready, 1)

            def store_x(t, pair, tiles):
                left(pool, pair, tiles)
                pool.tensor_copy(x[:, :, bass.ts(t, NT)], stage[:, :, :]).then_inc(x_stored, 1)

            norm(0, 0)

            def head_norms(g):
                head_norm(2 * g, HD ** -0.5, NORM_STEPS + 2 * g * HEAD_STEPS, 1, A_P1 + g)
                head_norm(2 * g + 1, 1.0, NORM_STEPS + (2 * g + 1) * HEAD_STEPS, 0, A_P0 + 2 * g + 1)

            for g in range(GROUPS):
                head_norms(g)
            heads_end = NORM_STEPS + 2 * GROUPS * HEAD_STEPS
            for t in range(XN):
                store_x(t, *B_LEFT[t])
            norm(1, heads_end)
            with pool.Fori(0, XN) as t:
                store_x(t, 0, D_P0 + t + 1)
            norm(2, heads_end + NORM_STEPS)

        @block.scalar
        def _(act):
            for j in range(XN):
                act.dma_start(x[:, :, j * NT:(j + 1) * NT],
                              x_in[0, :, j * NT:(j + 1) * NT].rearrange("(t p) n -> p t n", p=P)).then_inc(x_loaded[j], 16)
                if j == 0:
                    for i, g in enumerate((g_mix, g_ffn, g_ple)):
                        act.dma_start(gain_rows[i * KD:(i + 1) * KD, :],
                                      g[0, :].rearrange("(c p) -> c p", p=P)).then_inc(gains_loaded, 16)
                    for i, g in enumerate((g_q, g_k)):
                        act.dma_start(gain_rows[3 * KD + i:3 * KD + i + 1, :], g).then_inc(gains_loaded, 16)
            act.dma_start(p_sb[:, :, :], p_in[0, 0].rearrange("(t p) n -> p t n", p=P)).then_inc(p_loaded, 16)

            def hi(U, u, n):
                act.wait_ge(landed[slot(u)], 16 * (U // RING + 1) if isinstance(U, int) else U * (16 // RING) + 16 - slot(u) * (16 // RING))
                if not isinstance(U, int) or U >= RING:
                    act.wait_ge(unit_used, U - RING + 1)
                act.activation(w_parts[0][:, slot(u), 0:n, :], raw[:, slot(u), 0:n, :], ACT.Copy).then_inc(hi_ready, 1)

            def turn_x(first, gain, rounds, banks):
                for i, (r, b) in enumerate(zip(rounds, banks)):
                    act.wait_ge(T_ready, r + 1)
                    for k in range(2):
                        c = first + 2 * i + k
                        last = act.activation(xT[0][:, c, :], T[b][:, k, :], ACT.Copy, scale=gains[:, gain + c:gain + c + 1])
                    last.then_inc(turned_hi, 1)

            def turn_tile(t, gain, k):
                for b in range(2):
                    act.wait_ge(T_ready, SETS0 + 2 * k + b + 1)
                    for i in range(2):
                        c = t * CB + 2 * b + i
                        last = act.activation(xT[0][:, bass.ds(c, 1), :].rearrange("p a s -> p (a s)"), T[b][:, i, :], ACT.Copy,
                                              scale=gains[:, bass.ds(gain + c, 1)])
                    last.then_inc(turned_hi, 1)

            def square_tile(t, pair, tiles, done):
                left(act, pair, tiles)
                for tb in range(TB):
                    act.wait_ge(x_ssq_ready, done * TB + tb)
                    act.activation(junk[:, :], stage[:, tb, :], ACT.Square,
                                   accum_out=x_ssq[:, bass.ds(t, 1), tb:tb + 1].rearrange("p a b -> p (a b)")).then_inc(x_ssq_ready, 1)

            def square_heads(U, tile, n, pair):
                act.wait_ge(head_ssq_ready, n)
                act.wait_ge(half_done, tile + 1)
                act.activation(squares[:, 0, :], acc[pair][0][:, :], ACT.Square)
                act.wait_ge(unit_used, U + 1)
                act.activation(squares[:, 1, :], acc[pair][1][:, :], ACT.Square).then_inc(squares_ready, 1)

            def turn_heads(to, gain, r, pair_of_heads):
                act.wait_ge(T_ready, X_ROUNDS + r + 1)
                act.activation(to[:, 2 * pair_of_heads:2 * pair_of_heads + 2, :], T[0][:, :, :], ACT.Copy,
                               scale=gains[:, gain:gain + 1]).then_inc(T_free[0], 1)

            def keep_v(g, U):
                for tb in range(TB):
                    if tb == 0:
                        act.wait_ge(half_done, 3 * g + 3)
                    else:
                        act.wait_ge(unit_used, U + 1)
                    act.activation(v[:, tb, :], acc[0][tb][:, :], ACT.Copy, scale=rstd[:, tb:tb + 1]).then_inc(acc_free[0][tb], 1)

            def softplus_of(h):
                act.wait_ge(z_ready, h + 1)
                act.wait_ge(log_1m_ready, h)
                act.wait_ge(log_sig_ready, h)
                act.activation(softplus[:, :], Z[:, 0:3 * P], ACT.Abs).then_inc(act_step, 1)
                act.wait_ge(act_step, 2 * h + 1)
                act.activation(softplus[:, :], softplus[:, :], ACT.Exp, scale=-1.0).then_inc(act_step, 1)
                act.wait_ge(act_step, 2 * h + 2)
                act.activation(softplus[:, :], softplus[:, :], ACT.Ln, bias=1.0).then_inc(softplus_ready, 1)

            def weights_of(h, even):
                act.wait_ge(exponent_ready, h + 1)
                act.activation(weight[even][:, :], weight[even][:, :], ACT.Exp).then_inc(weight_ready, 1)

            def keep_o(h):
                act.wait_ge(o_ready, h + 1)
                act.activation(oT[0][:, bass.ds(h, 1), :].rearrange("p a s -> p (a s)"), O[:, 0, :], ACT.Copy).then_inc(oT_hi_ready, 1)

            def attend(u, g):
                for h in range(HG):
                    if u == 2 * h + 7:
                        weights_of(g * HG + h, h % 2)
                for h in range(HG):
                    if u == 2 * h + 9:
                        keep_o(g * HG + h)
                for h in range(HG):
                    if u == 2 * h + 4:
                        softplus_of(g * HG + h)

            def group(g, first=False):
                U0 = A0 + g * AU
                for u in range(AU):
                    if first and u < DU:
                        act.wait_ge(gains_ready, 1)
                        turn_x(2 * u, MIX, [u], [u % 2])
                    if first and u == DU:
                        act.wait_ge(T_ready, X_ROUNDS)
                        act.activation(pT[0][:, :, :], T[0][:, :, :], ACT.Copy).then_inc(turned_hi, 1)
                    hi(U0 + u, u, 2)
                    if not first:
                        if u == 2:
                            keep_v(g - 1, U0 - 1)
                        attend(u, g - 1)
                    for part, (to, gain) in enumerate(((qT, QG), (kT, KG))):
                        end = (part + 1) * DU - 1
                        if u == end + 3:
                            square_heads(U0 + end, 3 * g + part, 2 * g + part, part)
                        if u == end + 8:
                            turn_heads(to, gain, 4 * g + 2 * part, 0)
                            if part == 1:
                                turn_heads(to, gain, 4 * g + 2 * part + 1, 1)
                        if u == end + 9 and part == 0:
                            turn_heads(to, gain, 4 * g + 1, 1)

            group(0, first=True)
            with act.Fori(1, GROUPS) as g:
                group(g)

            for u, (t, blocks) in enumerate(B_HEAD):
                hi(B0 + u, u, len(blocks))
                if u == 2:
                    keep_v(GROUPS - 1, B0 - 1)
                attend(u, GROUPS - 1)
            for u in range(DU):
                hi(B2 + u, u, 2)
                for t in range(2):
                    end = B_END[t] - BH
                    if u == end + 4:
                        square_tile(t, *B_LEFT[t], XN + t)
                    if u == end + 6:
                        turn_tile(t, FFN, t)
            for u in range(DU):
                hi(B2 + DU + u, u, 2)
                if u == 3:
                    square_tile(2, *B_LEFT[2], XN + 2)
                if u == 5:
                    turn_tile(2, FFN, 2)

            def turn_hidden(j, k):
                for b in range(2):
                    act.wait_ge(T_ready, SETS0 + 2 * k + b + 1)
                    act.activation(hT[0][:, bass.ds(j * CB + 2 * b, 2), :], T[b][:, :, :], ACT.Copy).then_inc(turned_hi, 1)

            def gate_up(j, first=False):
                U0 = C0 + j * CU
                for u in range(CU):
                    hi(U0 + u, u, 2)
                    if first and u == 3:
                        square_tile(XN - 1, *B_LEFT[XN - 1], 2 * XN - 1)
                    if u == 5:
                        if first:
                            turn_tile(XN - 1, FFN, XN - 1)
                        else:
                            turn_hidden(j - 1, C_SET + j)
                    if u == DU + 2:
                        act.wait_ge(rstd_ready, 2)
                        act.wait_ge(T_ready, SETS0 + 2 * (C_SET + j) + 2)
                        act.wait_ge(x_stored, XN)
                        for tb in range(TB):
                            if tb == 0:
                                act.wait_ge(half_done, TC + 2 * j + 1)
                            else:
                                act.wait_ge(unit_used, U0 + DU)
                            act.activation(stage[:, tb, :], acc[0][tb][:, :], ACT.Sigmoid,
                                           scale=rstd[:, tb:tb + 1]).then_inc(sig_ready, 1)

            gate_up(0, first=True)
            with act.Fori(1, FN) as j:
                gate_up(j)

            def down(n, first=False):
                for u in range(FU):
                    hi(D0 + n * FU + u, u, len(F_UNITS[u]))
                    if u == 3 and not first:
                        square_tile(n - 1, 0, D_P0 + n, 2 * XN + n - 1)
                    if u == 5:
                        if first:
                            turn_hidden(FN - 1, D_SET)
                        else:
                            turn_tile(n - 1, PLE, D_SET + n)

            down(0, first=True)
            with act.Fori(1, XN) as n:
                down(n)

            def gate_out(n, U):
                act.wait_ge(rstd_ready, 3)
                act.wait_ge(x_stored, 2 * XN)
                act.wait_ge(T_ready, SETS0 + 2 * E_SET + 2)
                act.wait_ge(x_final, n * TB)
                for tb in range(TB):
                    if tb == 0:
                        act.wait_ge(half_done, TE + 2 * n + 1)
                    else:
                        act.wait_ge(unit_used, U + 1)
                    act.activation(stage[:, tb, :], acc[0][tb][:, :], ACT.Sigmoid,
                                   scale=rstd[:, tb:tb + 1]).then_inc(acc_free[0][tb], 1)

            def store_out(n):
                for tb in range(TB):
                    act.wait_ge(x_final, n * TB + tb + 1)
                    act.dma_start(out[0, tb * P:(tb + 1) * P, :][:, bass.ts(n, NT)],
                                  x[:, tb, bass.ts(n, NT)]).then_inc(out_done, 16)

            def embed(n, first=False):
                U0 = E0 + n * EU
                for u in range(EU):
                    hi(U0 + u, u, len(G_UNITS[u]) if u < EU - 1 else KP)
                    if first and u == 3:
                        square_tile(XN - 1, 0, E_P0, 3 * XN - 1)
                    if first and u == 5:
                        turn_tile(XN - 1, PLE, E_SET)
                    if not first and u == 1:
                        gate_out(n - 1, U0 - 2)
                    if not first and u == 5:
                        store_out(n - 1)

            embed(0, first=True)
            with act.Fori(1, XN) as n:
                embed(n)
            gate_out(XN - 1, E0 + XN * EU - 2)
            store_out(XN - 1)
            act.wait_ge(out_done, 16 * XN * TB)

        @block.vector
        def _(dve):
            def lo(U, u, n):
                dve.wait_ge(hi_ready, U + 1)
                dve.tensor_tensor(w_parts[1][:, slot(u), 0:n, :], raw[:, slot(u), 0:n, :],
                                  w_parts[0][:, slot(u), 0:n, :].bitcast(F32), ALU.subtract).then_inc(lo_ready, 1)

            def turn_block(c, gain, b, k):
                return dve.scalar_tensor_tensor(
                    out=xT[1][:, bass.ds(c, 1), :].rearrange("p a s -> p (a s)"), in0=T[b][:, k, :],
                    scalar=gains[:, bass.ds(gain + c, 1)],
                    in1=xT[0][:, bass.ds(c, 1), :].rearrange("p a s -> p (a s)").bitcast(F32),
                    op0=ALU.mult, op1=ALU.subtract)

            def turn_tile(t, gain, k):
                for b in range(2):
                    dve.wait_ge(turned_hi, X_ROUNDS + 2 * k + b + 1)
                    turn_block(t * CB + 2 * b, gain, b, 0)
                    turn_block(t * CB + 2 * b + 1, gain, b, 1).then_inc(T_free[b], 1)

            def sum_heads(n):
                dve.wait_ge(squares_ready, n + 1)
                dve.wait_ge(head_scale_ready, n)
                dve.reduce_sum(head_ssq[:, :], squares[:, :, :].rearrange("p t (h d) -> p (t h) d", d=HD),
                               AX_X).then_inc(head_ssq_ready, 1)

            def norm_heads(n, pair, rounds):
                dve.wait_ge(head_scale_ready, n + 1)
                dve.wait_ge(T_ready, X_ROUNDS + rounds)
                for tb in range(TB):
                    factor = head_scale[:, tb * HG:(tb + 1) * HG].unsqueeze(2).broadcast_to([P, HG, HD])
                    dve.tensor_tensor(normed[:, tb, :].rearrange("p (h d) -> p h d", d=HD),
                                      acc[pair][tb][:, :].rearrange("p (h d) -> p h d", d=HD),
                                      factor, ALU.mult).then_inc(acc_free[pair][tb], 1)

            def log_terms(h, even):
                dve.wait_ge(softplus_ready, h + 1)
                dve.wait_ge(rest_ready, h)
                dve.scalar_tensor_tensor(out=neg_log_1m[:, :], in0=Z[:, 0:3 * P], scalar=0.0, in1=softplus[:, :],
                                         op0=ALU.max, op1=ALU.add).then_inc(dve_step, 1)
                dve.scalar_tensor_tensor(out=weight[even][:, :], in0=Z[:, 0:3 * P], scalar=0.0, in1=softplus[:, :],
                                         op0=ALU.min, op1=ALU.subtract).then_inc(z_free, 1)
                dve.wait_ge(dve_step, h + 1)
                dve.tensor_tensor(diagonals(neg_log_1m), diagonals(neg_log_1m), seen[:, :, :],
                                  ALU.mult).then_inc(log_1m_ready, 1)
                dve.wait_ge(z_free, h + 1)
                dve.tensor_tensor(diagonals(weight[even]), diagonals(weight[even]), unseen[:, :, :],
                                  ALU.add).then_inc(log_sig_ready, 1)

            def exponent(h, even):
                dve.wait_ge(rest_ready, h + 1)
                dve.wait_ge(log_sig_ready, h + 1)
                dve.tensor_tensor(weight[even][:, :], weight[even][:, :], R[:, 0:3 * P], ALU.subtract).then_inc(exponent_ready, 1)

            def keep_o(h):
                dve.wait_ge(oT_hi_ready, h + 1)
                dve.tensor_tensor(oT[1][:, bass.ds(h, 1), :].rearrange("p a s -> p (a s)"), O[:, 0, :],
                                  oT[0][:, bass.ds(h, 1), :].rearrange("p a s -> p (a s)").bitcast(F32),
                                  ALU.subtract).then_inc(oT_ready, 1)

            def attend(u, g):
                for h in range(HG):
                    if u == 2 * h + 6:
                        exponent(g * HG + h, h % 2)
                for h in range(HG):
                    if u == 2 * h + 4:
                        log_terms(g * HG + h, h % 2)
                for h in range(HG):
                    if u == 2 * h + 9:
                        keep_o(g * HG + h)

            def group(g, first=False):
                U0 = A0 + g * AU
                for u in range(AU):
                    if first and u < DU:
                        dve.wait_ge(turned_hi, u + 1)
                        turn_block(2 * u, MIX, u % 2, 0)
                        turn_block(2 * u + 1, MIX, u % 2, 1).then_inc(T_free[u % 2], 1)
                    if first and u == DU:
                        dve.wait_ge(turned_hi, X_ROUNDS)
                        dve.tensor_tensor(pT[1][:, :, :], T[0][:, :, :], pT[0][:, :, :].bitcast(F32),
                                          ALU.subtract).then_inc(T_free[0], 1)
                    lo(U0 + u, u, 2)
                    if first and u < DU:
                        t, tb = u // 2, u % 2
                        dve.wait_ge(x_loaded[t], 16)
                        dve.wait_ge(x_ssq_ready, u)
                        part = x[:, tb, t * NT:(t + 1) * NT]
                        dve.tensor_tensor_reduce(junk[:, :], part, part, 1.0, 0.0, ALU.mult, ALU.add,
                                                 x_ssq[:, t, tb:tb + 1]).then_inc(x_ssq_ready, 1)
                    if not first:
                        attend(u, g - 1)
                    for part in range(2):
                        end = (part + 1) * DU - 1
                        if u == end + 3:
                            sum_heads(2 * g + part)
                        if u == end + 6:
                            norm_heads(2 * g + part, part, 4 * g + 2 * part)

            dve.wait_ge(gains_turned, 1)
            dve.tensor_copy(gains[:, :], Z[:, 0:3 * KD + 2]).then_inc(gains_ready, 1)
            dve.wait_ge(gains_ready, 1)
            group(0, first=True)
            with dve.Fori(1, GROUPS) as g:
                group(g)

            def add_residual(t, tile, U, pair, k, stores):
                dve.wait_ge(T_ready, SETS0 + 2 * k)
                dve.wait_ge(x_stored, stores)
                dve.wait_ge(x_ssq_ready, (stores + XN) * TB)
                for tb in range(TB):
                    if tb == 0:
                        dve.wait_ge(half_done, tile + 1)
                    else:
                        dve.wait_ge(unit_used, U + 1)
                    dve.tensor_tensor(stage[:, tb, :], acc[pair][tb][:, :], x[:, tb, bass.ts(t, NT)],
                                      ALU.add).then_inc(acc_free[pair][tb], 1)

            for u, (t, blocks) in enumerate(B_HEAD):
                lo(B0 + u, u, len(blocks))
                attend(u, GROUPS - 1)
            for u in range(DU):
                lo(B2 + u, u, 2)
                for t in range(2):
                    end = B_END[t] - BH
                    if u == end + 3:
                        add_residual(t, TBO + t, B2 + end, t, t, t)
                    if u == end + 6:
                        turn_tile(t, FFN, t)
            for u in range(DU):
                lo(B2 + DU + u, u, 2)
                if u == 2:
                    add_residual(2, TBO + 2, B2 + DU - 1, 0, 2, 2)
                if u == 5:
                    turn_tile(2, FFN, 2)

            def turn_hidden(j, k):
                for b in range(2):
                    dve.wait_ge(turned_hi, X_ROUNDS + 2 * k + b + 1)
                    dve.tensor_tensor(hT[1][:, bass.ds(j * CB + 2 * b, 2), :], T[b][:, :, :],
                                      hT[0][:, bass.ds(j * CB + 2 * b, 2), :].bitcast(F32), ALU.subtract).then_inc(T_free[b], 1)

            def times_up(j, U):
                for tb in range(TB):
                    dve.wait_ge(acc_free[0][tb], C_P0 + j + 1)
                    if tb == 0:
                        dve.wait_ge(half_done, TC + 2 * j + 2)
                    else:
                        dve.wait_ge(unit_used, U + 1)
                    dve.tensor_tensor(stage[:, tb, :], stage[:, tb, :], acc[1][tb][:, :], ALU.mult).then_inc(acc_free[1][tb], 1)

            def gate_up(j, first=False):
                U0 = C0 + j * CU
                for u in range(CU):
                    lo(U0 + u, u, 2)
                    if u == 2:
                        if first:
                            add_residual(XN - 1, TBO + XN - 1, C0 - 1, 0, XN - 1, XN - 1)
                        else:
                            times_up(j - 1, U0 - 1)
                    if u == 5:
                        if first:
                            turn_tile(XN - 1, FFN, XN - 1)
                        else:
                            turn_hidden(j - 1, C_SET + j)
                    if u == DU + 2:
                        for tb in range(TB):
                            dve.wait_ge(sig_ready, TB * j + tb + 1)
                            dve.scalar_tensor_tensor(out=stage[:, tb, :], in0=acc[0][tb][:, :], scalar=rstd2[:, tb:tb + 1],
                                                     in1=stage[:, tb, :], op0=ALU.mult, op1=ALU.mult).then_inc(acc_free[0][tb], 1)

            gate_up(0, first=True)
            with dve.Fori(1, FN) as j:
                gate_up(j)

            def down(n, first=False):
                for u in range(FU):
                    lo(D0 + n * FU + u, u, len(F_UNITS[u]))
                    if u == 2:
                        if first:
                            times_up(FN - 1, D0 - 1)
                        else:
                            add_residual(n - 1, TD + n - 1, D0 + n * FU - 1, 0, D_SET + n, XN + n - 1)
                    if u == 5:
                        if first:
                            turn_hidden(FN - 1, D_SET)
                        else:
                            turn_tile(n - 1, PLE, D_SET + n)

            down(0, first=True)
            with dve.Fori(1, XN) as n:
                down(n)

            def add_embedding(n, U):
                for tb in range(TB):
                    dve.wait_ge(acc_free[0][tb], E_P0 + n + 1)
                    if tb == 0:
                        dve.wait_ge(half_done, TE + 2 * n + 2)
                    else:
                        dve.wait_ge(unit_used, U + 1)
                    dve.tensor_tensor(stage[:, tb, :], stage[:, tb, :], acc[1][tb][:, :], ALU.mult).then_inc(acc_free[1][tb], 1)
                for tb in range(TB):
                    dve.wait_ge(acc_free[1][tb], E_P1 + n + 1)
                    part = x[:, tb, bass.ts(n, NT)]
                    dve.tensor_tensor(part, part, stage[:, tb, :], ALU.add).then_inc(x_final, 1)

            def embed(n, first=False):
                U0 = E0 + n * EU
                for u in range(EU):
                    lo(U0 + u, u, len(G_UNITS[u]) if u < EU - 1 else KP)
                    if u == 2:
                        if first:
                            add_residual(XN - 1, TD + XN - 1, E0 - 1, 0, E_SET, 2 * XN - 1)
                        else:
                            add_embedding(n - 1, U0 - 1)
                    if first and u == 5:
                        turn_tile(XN - 1, PLE, E_SET)

            embed(0, first=True)
            with dve.Fori(1, XN) as n:
                embed(n)
            add_embedding(XN - 1, E0 + XN * EU - 1)

        @block.tensor
        def _(pe):
            def products(U, u, parts, blocks, pair, start, stop, before):
                pe.wait_ge(lo_ready, U + 1)
                for tb in range(TB):
                    if start:
                        pe.wait_ge(acc_free[pair][tb], before)
                    for i, c in enumerate(blocks):
                        for n, (a, w) in enumerate(((0, 0), (0, 1), (1, 0))):
                            last = pe.matmul(acc[pair][tb][:, :], parts[a][:, c, tb * P:(tb + 1) * P],
                                             w_parts[w][:, slot(u), i, :],
                                             start=(start and i == 0 and n == 0),
                                             stop=(stop and i == len(blocks) - 1 and n == 2))
                    if tb == TB - 1:
                        last.then_inc(unit_used, 1)
                    elif stop:
                        last.then_inc(half_done, 1)

            def turn(b, source, pairs, before):
                pe.wait_ge(T_free[b], before)
                for k in range(2):
                    for tb in range(TB):
                        last = pe.transpose(T[b][:, k, tb * P:(tb + 1) * P],
                                            source[:, tb, (pairs + k) * P:(pairs + k + 1) * P], ident[:, :])
                last.then_inc(T_ready, 1)

            def turn_stage(k, *stages):
                for pair, tiles in stages:
                    left(pe, pair, tiles)
                turn(0, stage, 0, SETS0_T0 + k)
                turn(1, stage, 2, SETS0_T1 + k)

            def scores(h, in_group, g):
                pe.wait_ge(T_free[0], (X_ROUNDS + 1) // 2 + 4 * (g + 1))
                pe.wait_ge(z_free, h)
                pe.matmul(Z[:, 0:2 * P], kT[:, in_group, 0:P], qT[:, in_group, :], start=True, stop=True)
                pe.matmul(Z[:, 2 * P:3 * P], kT[:, in_group, P:2 * P], qT[:, in_group, P:2 * P],
                          start=True, stop=True).then_inc(z_ready, 1)

            def rest(h):
                pe.wait_ge(log_1m_ready, h + 1)
                pe.wait_ge(exponent_ready, h)
                pe.matmul(R[:, 0:3 * P], later[:, :], neg_log_1m[:, :], start=True, stop=False)
                pe.matmul(R[:, P:2 * P], ones[:, :], neg_log_1m[:, 2 * P:3 * P], start=False, stop=True).then_inc(rest_ready, 1)

            def weigh(h, in_group, g):
                pe.wait_ge(weight_ready, h + 1)
                left(pe, 0, A_P0 + 2 * (g + 1))
                pe.wait_ge(oT_ready, h)
                w = weight[in_group % 2]
                head = slice(in_group * HD, (in_group + 1) * HD)
                pe.matmul(O[:, 0, :], v[:, 0, head], w[:, 0:2 * P], start=True, stop=False)
                pe.matmul(O[:, 0, P:2 * P], v[:, 1, head], w[:, 2 * P:3 * P], start=False, stop=True).then_inc(o_ready, 1)

            def attend(u, g):
                for h in range(HG):
                    if u == 2 * h + 5:
                        weigh(g * HG + h, h, g)
                for h in range(HG):
                    if u == 2 * h + 3:
                        rest(g * HG + h)
                for h in range(HG):
                    if u == 2 * h + 1:
                        scores(g * HG + h, h, g)

            def turn_input(r):
                if r < KD // 2:
                    pe.wait_ge(x_loaded[r * 2 // CB], 16)
                    turn(r % 2, x, 2 * r, r // 2)
                else:
                    pe.wait_ge(p_loaded, 16)
                    turn(0, p_sb, 0, r // 2)

            def group(g, first=False):
                U0 = A0 + g * AU
                for u in range(AU):
                    part, k = divmod(u, DU)
                    if first and u < DU:
                        if u + 2 < X_ROUNDS:
                            turn_input(u + 2)
                        pe.wait_ge(T_free[u % 2], u // 2 + 1)
                    if not first:
                        attend(u, g - 1)
                    for i in range(2):
                        for m in range(2):
                            if u == (i + 1) * DU + 4 + m:
                                left(pe, i, (A_P0 + 2 * g, A_P1 + g)[i] + 1)
                                turn(0, normed, 2 * m, (X_ROUNDS + 1) // 2 + 4 * g + 2 * i + m)
                    before = A_P1 + g if part == 1 else A_P0 + 2 * g + part // 2
                    products(U0 + u, u, xT, D_UNITS[k], part % 2, k == 0, k == DU - 1, before)

            pe.wait_ge(consts_ready, 4)
            pe.wait_ge(gains_loaded, 16 * 5)
            pe.transpose(Z[:, 0:3 * KD + 2], gain_rows[:, :], ident[0:3 * KD + 2, 0:3 * KD + 2]).then_inc(gains_turned, 1)
            turn_input(0)
            turn_input(1)
            group(0, first=True)
            with pe.Fori(1, GROUPS) as g:
                group(g)

            for u, (t, blocks) in enumerate(B_HEAD):
                attend(u, GROUPS - 1)
                if blocks[-1] >= HEADS - HG:
                    pe.wait_ge(oT_ready, blocks[-1] + 1)
                products(B0 + u, u, oT, blocks, t, blocks[0] == 0, blocks[-1] == KD - 1, (B_P0, B_P1)[t])
            for n in range(XN - 2):
                for u in range(DU):
                    if n == 0 and u in (0, 2):
                        turn_stage(u // 2, B_LEFT[u // 2])
                    if n == 1 and u == 2:
                        turn_stage(2, B_LEFT[2])
                    products(B2 + n * DU + u, u, oT, D_UNITS[u], 0, u == 0, u == DU - 1, B_P0 + 1 + n)

            with pe.Fori(0, FN) as j:
                for u in range(CU):
                    part, k = divmod(u, DU)
                    if u == 2:
                        turn_stage(C_SET + j, (0, C_P0), (1, C_P1 + j))
                    if part == 0:
                        pe.wait_ge(T_free[k % 2], rounds_of_set(k // 2)[k % 2])
                    products(C0 + j * CU + u, u, xT, D_UNITS[k], part, k == 0, k == DU - 1, (C_P0, C_P1)[part] + j)

            with pe.Fori(0, XN) as n:
                for u in range(FU):
                    for b in range(2):
                        if u == 0:
                            pe.wait_ge(T_free[b], rounds_of_set(D_SET - 1)[b])
                        if F_UNITS[u][0] == KF - CB:
                            pe.wait_ge(T_free[b], rounds_of_set(D_SET)[b])
                    if u == 2:
                        turn_stage(D_SET + n, (1, E_P1), (0, D_P0 + n))
                    products(D0 + n * FU + u, u, hT, F_UNITS[u], 0, u == 0, u == FU - 1, D_P0 + n)

            def embed(n, first=False):
                for u in range(EU):
                    U = E0 + n * EU + u
                    if first and u == 2:
                        turn_stage(E_SET, (0, E_P0))
                    if u < EU - 1:
                        if first:
                            t, b = divmod(G_UNITS[u][-1] // 2, 2)
                            pe.wait_ge(T_free[b], rounds_of_set(D_SET + 1 + t)[b])
                        products(U, u, xT, G_UNITS[u], 0, u == 0, u == EU - 2, E_P0 + n)
                    else:
                        products(U, u, pT, list(range(KP)), 1, True, True, E_P1 + n)

            embed(0, first=True)
            with pe.Fori(1, XN) as n:
                embed(n)


_INS = ["x", "p", "norm_mix", "norm_ffn", "sb_w_in", "sb_q_gain", "sb_k_gain", "sb_w_out",
        "ffn_w_gate", "ffn_w_up", "ffn_w_down", "ple_norm", "ple_w_gate", "ple_w_proj"]
_FLAT = ("sb_w_in", "sb_w_out", "ffn_w_gate", "ffn_w_up", "ffn_w_down", "ple_w_gate", "ple_w_proj")


def kernel(**inputs):
    import concourse.bacc as bacc
    from concourse.bass_utils import run_bass_kernel_spmd

    nc = bacc.Bacc("TRN2", target_bir_lowering=False, num_devices=1)
    arrays, args = {}, []
    for name in _INS:
        a = np.ascontiguousarray(inputs[name])
        if name in _FLAT:
            a = a.reshape(a.shape[1:])
        arrays[f"in_{name}"] = a
        args.append(nc.dram_tensor(f"in_{name}", a.shape, mybir.dt.from_np(a.dtype), kind="ExternalInput").ap())
    out = nc.dram_tensor("out_0", inputs["x"].shape, F32, kind="ExternalOutput").ap()
    trunk(nc, *args, out)
    r = run_bass_kernel_spmd(nc, [arrays], core_ids=[0])
    return r.results[0]["out_0"]
```

```python
from contextlib import ExitStack

import numpy as np
import concourse.bass as bass
from concourse import mybir

F32 = mybir.dt.float32
F32R = mybir.dt.float32r
ACT = mybir.ActivationFunctionType
ALU = mybir.AluOpType
AX_X = mybir.AxisListType.X

P = 128
NT = 512
WARM = 4, 9
RING = 4
EPS = 1e-6
MASKED = -1e30


def trunk(nc, x_in, p_in, g_mix, g_ffn, w_in, g_q, g_k, w_o, w_gate, w_up, w_down, g_ple, w_pg, w_pp, out):
    _, SEQ, D = x_in.shape
    TB = SEQ // P
    KD = D // P
    FF = w_gate.shape[1]
    KF = FF // P
    KP = w_pp.shape[0] // P
    HD = g_q.shape[1]
    HEADS = D // HD
    HG = NT // HD
    GROUPS = HEADS // HG
    XN = D // NT
    FN = FF // NT
    CB = NT // P
    assert TB == 2 and HD == P and D % NT == 0 and FF % NT == 0 and KP == 2 and KD == 16 and HG == 4

    D_UNITS = [[2 * i, 2 * i + 1] for i in range(KD // 2)]
    F_UNITS = ([[2 * i, 2 * i + 1] for i in range(6)] + [[c] for c in range(12, 16)]
               + [[2 * i, 2 * i + 1] for i in range(8, KF // 2)])
    G_UNITS = [[2 * i, 2 * i + 1] for i in range(5)] + [[c] for c in range(10, KD)]
    DU, FU, EU = len(D_UNITS), len(F_UNITS), len(G_UNITS) + 1
    AU = 3 * DU
    CU = 2 * DU
    B_HEAD = [(t, D_UNITS[u]) for t in range(2) for u in range(6)] + [(t, D_UNITS[u]) for t in range(2) for u in (6, 7)]
    BH = len(B_HEAD)
    B_END = [B_HEAD.index((t, D_UNITS[7])) for t in range(2)]
    assert all(n % RING == 0 for n in (AU, CU, FU, EU, BH, DU))
    A0 = 0
    B0 = A0 + GROUPS * AU
    B2 = B0 + BH
    C0 = B2 + (XN - 2) * DU
    D0 = C0 + FN * CU
    E0 = D0 + XN * FU
    TA, TBO = 0, 3 * GROUPS
    TC = TBO + XN
    TD = TC + 2 * FN
    TE = TD + XN
    A_P0, A_P1 = 0, 0
    B_P0, B_P1 = 2 * GROUPS, GROUPS
    C_P0, C_P1 = B_P0 + XN - 1, B_P1 + 1
    D_P0 = C_P0 + FN
    E_P0, E_P1 = D_P0 + XN, C_P1 + FN
    X_ROUNDS = KD // 2 + 1
    B_LEFT = [(0, B_P0 + 1), (1, B_P1 + 1), (0, B_P0 + 2), (0, B_P0 + 3)]
    SETS0 = X_ROUNDS + 4 * GROUPS
    SETS0_T0, SETS0_T1 = (X_ROUNDS + 1) // 2 + 4 * GROUPS, X_ROUNDS // 2
    C_SET, D_SET, E_SET = XN - 1, XN - 1 + FN, XN - 1 + FN + XN

    A_EVERY, B_EVERY = 3, 2
    R_AT, W_AT = 3, 6

    with ExitStack() as ctx:
        def sb(name, shape, dt=F32, where=ctx):
            return where.enter_context(nc.sbuf_tensor(name, shape, dt))

        def sem(name):
            return ctx.enter_context(nc.semaphore(name))

        x = sb("x", [P, TB, D])
        xT = [sb("xT_hi", [P, KD, SEQ], F32R), sb("xT_lo", [P, KD, SEQ], F32R)]
        pT = [sb("pT_hi", [P, KP, SEQ], F32R), sb("pT_lo", [P, KP, SEQ], F32R)]
        raw = sb("raw", [P, RING, 2, NT])
        w_parts = [sb("w_hi", [P, RING, 2, NT], F32R), sb("w_lo", [P, RING, 2, NT], F32R)]
        stage = sb("stage", [P, TB, NT])
        junk = sb("junk", [P, NT])
        early = sb("early", [P, 1])
        ident = sb("ident", [P, P])
        gains = sb("gains", [P, 3 * KD + 2])
        MIX, FFN, PLE, QG, KG = 0, KD, 2 * KD, 3 * KD, 3 * KD + 1
        x_ssq = sb("x_ssq", [P, XN, TB])
        pair_sum = sb("pair_sum", [P, 2, TB])
        mean_sq = sb("mean_sq", [P, TB])
        newton = sb("newton", [P, TB * HG])
        rstd = sb("rstd", [P, TB])
        rstd2 = sb("rstd2", [P, TB])
        head_ssq = sb("head_ssq", [P, TB * HG])
        head_ms = sb("head_ms", [P, TB * HG])
        head_r = sb("head_r", [P, TB * HG])
        head_scale = sb("head_scale", [P, TB * HG])
        minus_half = sb("minus_half", [P, TB * HG])
        with ExitStack() as attention:
            def at(name, shape, dt=F32):
                return sb(name, shape, dt, attention)
            oT = [at("oT_hi", [P, HEADS, SEQ], F32R), at("oT_lo", [P, HEADS, SEQ], F32R)]
            squares = at("squares", [P, TB, NT])
            normed = at("normed", [P, TB, NT])
            qT = [at("qT_hi", [P, HG, SEQ], F32R), at("qT_lo", [P, HG, SEQ], F32R)]
            kT = [at("kT_hi", [P, HG, SEQ], F32R), at("kT_lo", [P, HG, SEQ], F32R)]
            v = [at("v_hi", [P, TB, NT], F32R), at("v_lo", [P, TB, NT], F32R)]
            softplus = at("softplus", [P, 3 * P])
            neg_log_1m = at("neg_log_1m", [P, 3 * P])
            neg_parts = [[at(f"neg{i}_hi", [P, 3 * P], F32R), at(f"neg{i}_lo", [P, 3 * P], F32R)] for i in range(2)]
            weight = [at(f"weight{i}", [P, 3 * P]) for i in range(HG)]
            weight_parts = [[at(f"weight{i}_hi", [P, 3 * P], F32R), at(f"weight{i}_lo", [P, 3 * P], F32R)] for i in range(2)]
            masks = at("masks", [P, 3, P])
            later = at("later", [P, P], F32R)
            ones = at("ones", [P, P], F32R)
            unseen = at("unseen", [P, 2, P], F32R)
            ident_r = at("ident_r", [P, P], F32R)
            mix_rows = at("mix_rows", [KD, P])
            gain_rows = at("gain_rows", [2 * KD + 2, P])
            p_sb = at("p_sb", [P, TB, KP * P])
        hT = [sb("hT_hi", [P, KF, SEQ], F32R), sb("hT_lo", [P, KF, SEQ], F32R)]

        acc = [[ctx.enter_context(nc.psum_tensor(f"acc{i}{tb}", [P, NT], F32)) for tb in range(TB)] for i in range(2)]
        Z = ctx.enter_context(nc.psum_tensor("Z", [P, NT], F32))
        R = ctx.enter_context(nc.psum_tensor("R", [P, NT], F32))
        T = [ctx.enter_context(nc.psum_tensor(f"T{i}", [P, 2, SEQ], F32)) for i in range(2)]
        O = T[1]

        landed = [sem(f"landed{s}") for s in range(RING)]
        hi_ready = sem("hi_ready")
        lo_ready = sem("lo_ready")
        unit_used = sem("unit_used")
        half_done = sem("half_done")
        acc_free = [[sem(f"acc_free{i}{tb}") for tb in range(TB)] for i in range(2)]
        x_loaded = [sem(f"x_loaded{r}") for r in range(KD // 2)]
        p_loaded = sem("p_loaded")
        mix_loaded = sem("mix_loaded")
        gains_loaded = sem("gains_loaded")
        zeroed = sem("zeroed")
        consts_ready = sem("consts_ready")
        parts_ready = sem("parts_ready")
        gains_turned = sem("gains_turned")
        gains_ready = sem("gains_ready")
        T_ready = sem("T_ready")
        T_free = [sem("T_free0"), sem("T_free1")]
        turned_hi = sem("turned_hi")
        x_ssq_ready = sem("x_ssq_ready")
        rstd_ready = sem("rstd_ready")
        pool_step = sem("pool_step")
        squares_ready = sem("squares_ready")
        head_ssq_ready = sem("head_ssq_ready")
        head_scale_ready = sem("head_scale_ready")
        z_ready = sem("z_ready")
        act_step = sem("act_step")
        softplus_ready = sem("softplus_ready")
        z_free = sem("z_free")
        log_1m_ready = sem("log_1m_ready")
        neg_hi_ready = sem("neg_hi_ready")
        neg_lo_ready = sem("neg_lo_ready")
        rest_ready = sem("rest_ready")
        exponent_ready = sem("exponent_ready")
        weight_ready = sem("weight_ready")
        weight_hi_ready = sem("weight_hi_ready")
        weight_lo_ready = sem("weight_lo_ready")
        v_hi_ready = sem("v_hi_ready")
        o_ready = sem("o_ready")
        oT_hi_ready = sem("oT_hi_ready")
        oT_ready = sem("oT_ready")
        x_stored = sem("x_stored")
        sig_ready = sem("sig_ready")
        x_final = sem("x_final")
        out_done = sem("out_done")

        def left(eng, pair, tiles):
            for tb in range(TB):
                eng.wait_ge(acc_free[pair][tb], tiles)

        def rounds_of_set(k):
            return SETS0_T0 + k + 1, SETS0_T1 + k + 1

        def slot(u):
            return u % RING

        block = ctx.enter_context(nc.Block())

        @block.sync
        def _(sp):
            def load(U, u, blocks, columns):
                n = len(blocks)
                if not isinstance(U, int) or U >= RING:
                    sp.wait_ge(lo_ready, U - RING + 1)
                src = columns[blocks[0] * P:(blocks[0] + n) * P, :].rearrange("(k p) n -> p k n", p=P)
                sp.dma_start(raw[:, slot(u), 0:n, :], src).then_inc(landed[slot(u)], 16)

            def group(g, skip=0):
                for part in range(skip, 3):
                    columns = w_in[:, part * D:(part + 1) * D][:, bass.ts(g, NT)]
                    for u in range(DU):
                        load(A0 + g * AU + part * DU + u, part * DU + u, D_UNITS[u], columns)

            def load_x(r):
                columns = slice(2 * r * P, (2 * r + 2) * P)
                sp.dma_start(x[:, :, columns], x_in[0, :, columns].rearrange("(t p) n -> p t n", p=P)).then_inc(x_loaded[r], 16)

            load_x(0)
            for u in range(DU):
                load(A0 + u, u, D_UNITS[u], w_in[:, 0:NT])
                if u == 0:
                    load_x(1)
                if u + 2 < DU:
                    load_x(u + 2)
            for i, g in enumerate((g_ffn, g_ple)):
                sp.dma_start(gain_rows[i * KD:(i + 1) * KD, :],
                             g[0, :].rearrange("(c p) -> c p", p=P)).then_inc(gains_loaded, 16)
            for i, g in enumerate((g_q, g_k)):
                sp.dma_start(gain_rows[2 * KD + i:2 * KD + i + 1, :], g).then_inc(gains_loaded, 16)
            sp.dma_start(p_sb[:, :, :], p_in[0, 0].rearrange("(t p) n -> p t n", p=P)).then_inc(p_loaded, 16)
            group(0, skip=1)
            with nc.Fori(1, GROUPS, engines=[mybir.EngineType.SP], hint_back_edge=True) as g:
                group(g)
            for u, (t, blocks) in enumerate(B_HEAD):
                load(B0 + u, u, blocks, w_o[:, t * NT:(t + 1) * NT])
            with nc.Fori(0, XN - 2, engines=[mybir.EngineType.SP], hint_back_edge=True) as n:
                for u in range(DU):
                    load(B2 + n * DU + u, u, D_UNITS[u], w_o[:, 2 * NT:][:, bass.ts(n, NT)])
            with nc.Fori(0, FN, engines=[mybir.EngineType.SP], hint_back_edge=True) as j:
                for part, w in enumerate((w_gate, w_up)):
                    for u in range(DU):
                        load(C0 + j * CU + part * DU + u, u, D_UNITS[u], w[:, bass.ts(j, NT)])
            with nc.Fori(0, XN, engines=[mybir.EngineType.SP], hint_back_edge=True) as n:
                for u in range(FU):
                    load(D0 + n * FU + u, u, F_UNITS[u], w_down[:, bass.ts(n, NT)])
            with nc.Fori(0, XN, engines=[mybir.EngineType.SP], hint_back_edge=True) as n:
                for u, blocks in enumerate(G_UNITS):
                    load(E0 + n * EU + u, u, blocks, w_pg[:, bass.ts(n, NT)])
                load(E0 + n * EU + EU - 1, EU - 1, list(range(KP)), w_pp[:, bass.ts(n, NT)])

        @block.gpsimd
        def _(pool):
            HALF_MS = TB * HG
            pool.memset(ident[:, :], 0.0).then_inc(zeroed, 1)
            pool.wait_ge(zeroed, 1)
            pool.affine_select(out=ident[:, :], in_=ident[:, :], compare_op=ALU.not_equal, fill=1.0,
                               base=0, pattern=[[-1, P]], channel_multiplier=1).then_inc(consts_ready, 1)
            pool.memset(masks[:, 0:2, :], 1.0).then_inc(zeroed, 1)
            pool.memset(masks[:, 2, :], 0.0).then_inc(zeroed, 1)
            pool.memset(minus_half[:, :], -0.5).then_inc(zeroed, 1)
            pool.wait_ge(zeroed, 4)
            pool.affine_select(out=masks[:, 0, :], in_=masks[:, 0, :], compare_op=ALU.is_gt, fill=0.0,
                               base=0, pattern=[[-1, P]], channel_multiplier=1).then_inc(consts_ready, 1)
            pool.affine_select(out=masks[:, 2, :], in_=masks[:, 2, :], compare_op=ALU.is_gt, fill=MASKED,
                               base=0, pattern=[[1, P]], channel_multiplier=-1).then_inc(consts_ready, 1)

            def inverse_root(r, ms, n, step):
                t = newton[:, 0:n]
                pool.wait_ge(pool_step, step)
                pool.tensor_tensor(r, ms, minus_half[:, 0:n], ALU.pow).then_inc(pool_step, 1)
                pool.wait_ge(pool_step, step + 1)
                pool.tensor_tensor(t, r, r, ALU.mult).then_inc(pool_step, 1)
                pool.wait_ge(pool_step, step + 2)
                pool.tensor_tensor(t, t, ms, ALU.mult).then_inc(pool_step, 1)
                pool.wait_ge(pool_step, step + 3)
                pool.tensor_scalar(t, t, -0.5, 1.5, ALU.mult, ALU.add).then_inc(pool_step, 1)
                pool.wait_ge(pool_step, step + 4)
                pool.tensor_tensor(r, r, t, ALU.mult).then_inc(pool_step, 1)

            NORM_STEPS = 8
            HEAD_STEPS = 9

            def norm(which, step):
                pool.wait_ge(x_ssq_ready, XN * TB * (which + 1))
                pool.tensor_tensor(pair_sum[:, :, :], x_ssq[:, 0:2, :], x_ssq[:, 2:4, :], ALU.add).then_inc(pool_step, 1)
                pool.wait_ge(pool_step, step + 1)
                pool.tensor_tensor(mean_sq[:, :], pair_sum[:, 0, :], pair_sum[:, 1, :], ALU.add).then_inc(pool_step, 1)
                pool.wait_ge(pool_step, step + 2)
                pool.tensor_scalar(mean_sq[:, :], mean_sq[:, :], 1.0 / D, EPS, ALU.mult, ALU.add).then_inc(pool_step, 1)
                inverse_root(rstd[:, :], mean_sq[:, :], TB, step + 3)
                pool.wait_ge(pool_step, step + 8)
                pool.tensor_tensor(rstd2[:, :], rstd[:, :], rstd[:, :], ALU.mult).then_inc(rstd_ready, 1)

            def head_norm(n, scale, step, pair_before, tiles_before):
                pool.wait_ge(head_ssq_ready, n + 1)
                pool.wait_ge(rstd_ready, 1)
                for tb in range(TB):
                    part = slice(tb * HG, (tb + 1) * HG)
                    pool.tensor_scalar(head_ms[:, part], head_ssq[:, part], rstd2[:, tb:tb + 1], 1.0 / HD,
                                       ALU.mult, ALU.mult).then_inc(pool_step, 1)
                pool.wait_ge(pool_step, step + 2)
                pool.tensor_scalar(head_ms[:, :], head_ms[:, :], EPS, 1.0, ALU.add, ALU.mult).then_inc(pool_step, 1)
                inverse_root(head_r[:, :], head_ms[:, :], HALF_MS, step + 3)
                pool.wait_ge(pool_step, step + 8)
                left(pool, pair_before, tiles_before)
                for tb in range(TB):
                    part = slice(tb * HG, (tb + 1) * HG)
                    last = pool.tensor_scalar(head_scale[:, part], head_r[:, part], rstd[:, tb:tb + 1], scale,
                                              ALU.mult, ALU.mult)
                    last.then_inc(pool_step if tb == 0 else head_scale_ready, 1)

            def store_x(t, pair, tiles):
                left(pool, pair, tiles)
                pool.tensor_copy(x[:, :, bass.ts(t, NT)], stage[:, :, :]).then_inc(x_stored, 1)

            norm(0, 0)

            def head_norms(g):
                head_norm(2 * g, HD ** -0.5, NORM_STEPS + 2 * g * HEAD_STEPS, 1, A_P1 + g)
                head_norm(2 * g + 1, 1.0, NORM_STEPS + (2 * g + 1) * HEAD_STEPS, 0, A_P0 + 2 * g + 1)

            for g in range(GROUPS):
                head_norms(g)
            heads_end = NORM_STEPS + 2 * GROUPS * HEAD_STEPS
            for t in range(XN):
                store_x(t, *B_LEFT[t])
            norm(1, heads_end)
            with nc.Fori(0, XN, engines=[mybir.EngineType.Pool], hint_back_edge=True) as t:
                store_x(t, 0, D_P0 + t + 1)
            norm(2, heads_end + NORM_STEPS)

        @block.scalar
        def _(act):
            act.dma_start(mix_rows[:, :], g_mix[0, :].rearrange("(c p) -> c p", p=P)).then_inc(mix_loaded, 16)

            act.wait_ge(consts_ready, 1)
            act.activation(early[:, :], ident[:, 0:1], ACT.Exp)

            def hi(U, u, n):
                act.wait_ge(landed[slot(u)], 16 * (U // RING + 1) if isinstance(U, int) else U * (16 // RING) + 16 - slot(u) * (16 // RING))
                if not isinstance(U, int) or U >= RING:
                    act.wait_ge(unit_used, U - RING + 1)
                act.activation(w_parts[0][:, slot(u), 0:n, :], raw[:, slot(u), 0:n, :], ACT.Copy).then_inc(hi_ready, 1)

            def turn_x(r):
                act.wait_ge(T_ready, r + 1)
                for k in range(2):
                    c = 2 * r + k
                    last = act.activation(xT[0][:, c, :], T[r % 2][:, k, :], ACT.Copy, scale=gains[:, MIX + c:MIX + c + 1])
                last.then_inc(turned_hi, 1)

            def turn_tile(t, gain, k):
                for b in range(2):
                    act.wait_ge(T_ready, SETS0 + 2 * k + b + 1)
                    for i in range(2):
                        c = t * CB + 2 * b + i
                        last = act.activation(xT[0][:, bass.ds(c, 1), :].rearrange("p a s -> p (a s)"), T[b][:, i, :], ACT.Copy,
                                              scale=gains[:, bass.ds(gain + c, 1)])
                    last.then_inc(turned_hi, 1)

            def square_tile(t, pair, tiles, done):
                left(act, pair, tiles)
                for tb in range(TB):
                    act.wait_ge(x_ssq_ready, done * TB + tb)
                    act.activation(junk[:, :], stage[:, tb, :], ACT.Square,
                                   accum_out=x_ssq[:, bass.ds(t, 1), tb:tb + 1].rearrange("p a b -> p (a b)")).then_inc(x_ssq_ready, 1)

            def square_heads(U, tile, n, pair):
                act.wait_ge(head_ssq_ready, n)
                act.wait_ge(half_done, tile + 1)
                act.activation(squares[:, 0, :], acc[pair][0][:, :], ACT.Square)
                act.wait_ge(unit_used, U + 1)
                act.activation(squares[:, 1, :], acc[pair][1][:, :], ACT.Square).then_inc(squares_ready, 1)

            def turn_heads(to, gain, r, pair_of_heads):
                act.wait_ge(T_ready, X_ROUNDS + r + 1)
                act.activation(to[0][:, 2 * pair_of_heads:2 * pair_of_heads + 2, :], T[0][:, :, :], ACT.Copy,
                               scale=gains[:, gain:gain + 1]).then_inc(turned_hi, 1)

            def keep_v(g, U):
                for tb in range(TB):
                    if tb == 0:
                        act.wait_ge(half_done, 3 * g + 3)
                    else:
                        act.wait_ge(unit_used, U + 1)
                    act.activation(v[0][:, tb, :], acc[0][tb][:, :], ACT.Copy, scale=rstd[:, tb:tb + 1]).then_inc(v_hi_ready, 1)

            def softplus_of(h):
                act.wait_ge(z_ready, h + 1)
                act.wait_ge(z_free, h)
                act.activation(softplus[:, :], Z[:, 0:3 * P], ACT.Abs).then_inc(act_step, 1)
                act.wait_ge(act_step, 2 * h + 1)
                act.activation(softplus[:, :], softplus[:, :], ACT.Exp, scale=-1.0).then_inc(act_step, 1)
                act.wait_ge(act_step, 2 * h + 2)
                act.activation(softplus[:, :], softplus[:, :], ACT.Ln, bias=1.0).then_inc(softplus_ready, 1)

            def weights_of(h, i):
                act.wait_ge(exponent_ready, h + 1)
                act.activation(weight[i][:, :], weight[i][:, :], ACT.Exp).then_inc(weight_ready, 1)
                act.wait_ge(weight_ready, h + 1)
                act.activation(weight_parts[i % 2][0][:, :], weight[i][:, :], ACT.Copy).then_inc(weight_hi_ready, 1)

            def keep_o(h):
                act.wait_ge(o_ready, h + 1)
                act.activation(oT[0][:, bass.ds(h, 1), :].rearrange("p a s -> p (a s)"), O[:, 0, :], ACT.Copy).then_inc(oT_hi_ready, 1)

            def attend(u, g, every):
                for h in range(HG):
                    if u == every * h + W_AT + 3:
                        keep_o(g * HG + h)
                    if u == every * h + R_AT + 4:
                        weights_of(g * HG + h, h)
                    if u == every * h + 3:
                        softplus_of(g * HG + h)

            def group(g, first=False):
                U0 = A0 + g * AU
                for u in range(AU):
                    if first and u < DU:
                        act.wait_ge(gains_ready, 1)
                        turn_x(u)
                    hi(U0 + u, u, 2)
                    if first and u == DU:
                        act.wait_ge(T_ready, X_ROUNDS)
                        act.activation(pT[0][:, :, :], T[0][:, :, :], ACT.Copy).then_inc(turned_hi, 1)
                    if first and u == DU + 2:
                        act.wait_ge(gains_ready, 2)
                    if not first:
                        if u == 1:
                            keep_v(g - 1, U0 - 1)
                        attend(u, g - 1, A_EVERY)
                    for part, (to, gain) in enumerate(((qT, QG), (kT, KG))):
                        end = (part + 1) * DU - 1
                        if u == end + 3:
                            square_heads(U0 + end, 3 * g + part, 2 * g + part, part)
                        if u == end + 8:
                            turn_heads(to, gain, 4 * g + 2 * part, 0)
                        if u == min(end + 10, AU - 1):
                            turn_heads(to, gain, 4 * g + 2 * part + 1, 1)

            group(0, first=True)
            with nc.Fori(1, GROUPS, engines=[mybir.EngineType.Activation], hint_back_edge=True) as g:
                group(g)

            for u, (t, blocks) in enumerate(B_HEAD):
                hi(B0 + u, u, len(blocks))
                if u == 1:
                    keep_v(GROUPS - 1, B0 - 1)
                attend(u, GROUPS - 1, B_EVERY)
            for u in range(DU):
                hi(B2 + u, u, 2)
                for t in range(2):
                    end = B_END[t] - BH
                    if u == end + 4:
                        square_tile(t, *B_LEFT[t], XN + t)
                    if u == end + 6:
                        turn_tile(t, FFN, t)
            for u in range(DU):
                hi(B2 + DU + u, u, 2)
                if u == 3:
                    square_tile(2, *B_LEFT[2], XN + 2)
                if u == 5:
                    turn_tile(2, FFN, 2)

            def turn_hidden(j, k):
                for b in range(2):
                    act.wait_ge(T_ready, SETS0 + 2 * k + b + 1)
                    act.activation(hT[0][:, bass.ds(j * CB + 2 * b, 2), :], T[b][:, :, :], ACT.Copy).then_inc(turned_hi, 1)

            def gate_up(j, first=False):
                U0 = C0 + j * CU
                for u in range(CU):
                    hi(U0 + u, u, 2)
                    if first and u == 3:
                        square_tile(XN - 1, *B_LEFT[XN - 1], 2 * XN - 1)
                    if u == 5:
                        if first:
                            turn_tile(XN - 1, FFN, XN - 1)
                        else:
                            turn_hidden(j - 1, C_SET + j)
                    if u == DU + 2:
                        act.wait_ge(rstd_ready, 2)
                        act.wait_ge(T_ready, SETS0 + 2 * (C_SET + j) + 2)
                        act.wait_ge(x_stored, XN)
                        for tb in range(TB):
                            if tb == 0:
                                act.wait_ge(half_done, TC + 2 * j + 1)
                            else:
                                act.wait_ge(unit_used, U0 + DU)
                            act.activation(stage[:, tb, :], acc[0][tb][:, :], ACT.Sigmoid,
                                           scale=rstd[:, tb:tb + 1]).then_inc(sig_ready, 1)

            gate_up(0, first=True)
            with nc.Fori(1, FN, engines=[mybir.EngineType.Activation], hint_back_edge=True) as j:
                gate_up(j)

            def down(n, first=False):
                for u in range(FU):
                    hi(D0 + n * FU + u, u, len(F_UNITS[u]))
                    if u == 3 and not first:
                        square_tile(n - 1, 0, D_P0 + n, 2 * XN + n - 1)
                    if u == 5:
                        if first:
                            turn_hidden(FN - 1, D_SET)
                        else:
                            turn_tile(n - 1, PLE, D_SET + n)

            down(0, first=True)
            with nc.Fori(1, XN, engines=[mybir.EngineType.Activation], hint_back_edge=True) as n:
                down(n)

            def gate_out(n, U):
                act.wait_ge(rstd_ready, 3)
                act.wait_ge(x_stored, 2 * XN)
                act.wait_ge(T_ready, SETS0 + 2 * E_SET + 2)
                act.wait_ge(x_final, n * TB)
                for tb in range(TB):
                    if tb == 0:
                        act.wait_ge(half_done, TE + 2 * n + 1)
                    else:
                        act.wait_ge(unit_used, U + 1)
                    act.activation(stage[:, tb, :], acc[0][tb][:, :], ACT.Sigmoid,
                                   scale=rstd[:, tb:tb + 1]).then_inc(acc_free[0][tb], 1)

            def store_out(n):
                for tb in range(TB):
                    act.wait_ge(x_final, n * TB + tb + 1)
                    act.dma_start(out[0, tb * P:(tb + 1) * P, :][:, bass.ts(n, NT)],
                                  x[:, tb, bass.ts(n, NT)]).then_inc(out_done, 16)

            def embed(n, first=False):
                U0 = E0 + n * EU
                for u in range(EU):
                    hi(U0 + u, u, len(G_UNITS[u]) if u < EU - 1 else KP)
                    if first and u == 3:
                        square_tile(XN - 1, 0, E_P0, 3 * XN - 1)
                    if first and u == 5:
                        turn_tile(XN - 1, PLE, E_SET)
                    if not first and u == 1:
                        gate_out(n - 1, U0 - 2)
                    if not first and u == 5:
                        store_out(n - 1)

            embed(0, first=True)
            with nc.Fori(1, XN, engines=[mybir.EngineType.Activation], hint_back_edge=True) as n:
                embed(n)
            gate_out(XN - 1, E0 + XN * EU - 2)
            store_out(XN - 1)
            act.wait_ge(out_done, 16 * XN * TB)

        @block.vector
        def _(dve):
            def lo(U, u, n):
                dve.wait_ge(hi_ready, U + 1)
                dve.tensor_tensor(w_parts[1][:, slot(u), 0:n, :], raw[:, slot(u), 0:n, :],
                                  w_parts[0][:, slot(u), 0:n, :].bitcast(F32), ALU.subtract).then_inc(lo_ready, 1)

            def turn_block(c, gain, b, k):
                return dve.scalar_tensor_tensor(
                    out=xT[1][:, bass.ds(c, 1), :].rearrange("p a s -> p (a s)"), in0=T[b][:, k, :],
                    scalar=gains[:, bass.ds(gain + c, 1)],
                    in1=xT[0][:, bass.ds(c, 1), :].rearrange("p a s -> p (a s)").bitcast(F32),
                    op0=ALU.mult, op1=ALU.subtract)

            def turn_tile(t, gain, k):
                for b in range(2):
                    dve.wait_ge(turned_hi, SETS0 + 2 * k + b + 1)
                    turn_block(t * CB + 2 * b, gain, b, 0)
                    turn_block(t * CB + 2 * b + 1, gain, b, 1).then_inc(T_free[b], 1)

            def sum_heads(n):
                dve.wait_ge(squares_ready, n + 1)
                dve.wait_ge(head_scale_ready, n)
                dve.reduce_sum(head_ssq[:, :], squares[:, :, :].rearrange("p t (h d) -> p (t h) d", d=HD),
                               AX_X).then_inc(head_ssq_ready, 1)

            def norm_heads(n, pair, rounds):
                dve.wait_ge(head_scale_ready, n + 1)
                dve.wait_ge(T_ready, X_ROUNDS + rounds)
                for tb in range(TB):
                    factor = head_scale[:, tb * HG:(tb + 1) * HG].unsqueeze(2).broadcast_to([P, HG, HD])
                    dve.tensor_tensor(normed[:, tb, :].rearrange("p (h d) -> p h d", d=HD),
                                      acc[pair][tb][:, :].rearrange("p (h d) -> p h d", d=HD),
                                      factor, ALU.mult).then_inc(acc_free[pair][tb], 1)

            def turn_heads(to, gain, r, pair_of_heads):
                part = slice(2 * pair_of_heads, 2 * pair_of_heads + 2)
                dve.wait_ge(turned_hi, X_ROUNDS + r + 1)
                dve.scalar_tensor_tensor(out=to[1][:, part, :], in0=T[0][:, :, :], scalar=gains[:, gain:gain + 1],
                                         in1=to[0][:, part, :].bitcast(F32), op0=ALU.mult,
                                         op1=ALU.subtract).then_inc(T_free[0], 1)

            def keep_v(g):
                for tb in range(TB):
                    dve.wait_ge(v_hi_ready, TB * g + tb + 1)
                    dve.scalar_tensor_tensor(out=v[1][:, tb, :], in0=acc[0][tb][:, :], scalar=rstd[:, tb:tb + 1],
                                             in1=v[0][:, tb, :].bitcast(F32), op0=ALU.mult,
                                             op1=ALU.subtract).then_inc(acc_free[0][tb], 1)

            def log_terms(h, i):
                neg = neg_parts[i % 2]
                dve.wait_ge(softplus_ready, h + 1)
                dve.wait_ge(neg_lo_ready, h)
                dve.scalar_tensor_tensor(out=neg_log_1m[:, :], in0=Z[:, 0:3 * P], scalar=0.0, in1=softplus[:, :],
                                         op0=ALU.max, op1=ALU.add).then_inc(log_1m_ready, 1)
                dve.scalar_tensor_tensor(out=weight[i][:, :], in0=Z[:, 0:3 * P], scalar=0.0, in1=softplus[:, :],
                                         op0=ALU.min, op1=ALU.subtract).then_inc(z_free, 1)
                dve.wait_ge(log_1m_ready, h + 1)
                dve.tensor_copy(neg[0][:, :], neg_log_1m[:, :]).then_inc(neg_hi_ready, 1)
                dve.wait_ge(neg_hi_ready, h + 1)
                dve.tensor_tensor(neg[1][:, :], neg_log_1m[:, :], neg[0][:, :].bitcast(F32),
                                  ALU.subtract).then_inc(neg_lo_ready, 1)

            def exponent(h, i):
                dve.wait_ge(rest_ready, h + 1)
                dve.wait_ge(z_free, h + 1)
                dve.tensor_tensor(weight[i][:, :], weight[i][:, :], R[:, 0:3 * P], ALU.subtract).then_inc(exponent_ready, 1)

            def weights_lo(h, i):
                dve.wait_ge(weight_hi_ready, h + 1)
                parts = weight_parts[i % 2]
                dve.tensor_tensor(parts[1][:, :], weight[i][:, :], parts[0][:, :].bitcast(F32),
                                  ALU.subtract).then_inc(weight_lo_ready, 1)

            def keep_o(h):
                dve.wait_ge(oT_hi_ready, h + 1)
                dve.tensor_tensor(oT[1][:, bass.ds(h, 1), :].rearrange("p a s -> p (a s)"), O[:, 0, :],
                                  oT[0][:, bass.ds(h, 1), :].rearrange("p a s -> p (a s)").bitcast(F32),
                                  ALU.subtract).then_inc(oT_ready, 1)

            def attend(u, g, every):
                for h in range(HG):
                    if u == every * h + W_AT + 3:
                        keep_o(g * HG + h)
                    if u == every * h + R_AT + 4:
                        weights_lo(g * HG + h, h)
                    if u == every * h + R_AT + 3:
                        exponent(g * HG + h, h)
                    if u == every * h + 3:
                        log_terms(g * HG + h, h)

            def group(g, first=False):
                U0 = A0 + g * AU
                for u in range(AU):
                    if first and u < DU:
                        dve.wait_ge(turned_hi, u + 1)
                        turn_block(2 * u, MIX, u % 2, 0)
                        turn_block(2 * u + 1, MIX, u % 2, 1).then_inc(T_free[u % 2], 1)
                    lo(U0 + u, u, 2)
                    if first and u == DU + 1:
                        dve.wait_ge(gains_turned, 2)
                        dve.tensor_copy(gains[:, KD:], Z[:, KD:3 * KD + 2]).then_inc(gains_ready, 1)
                        dve.wait_ge(gains_ready, 2)
                    if first and u == DU:
                        dve.wait_ge(turned_hi, X_ROUNDS)
                        dve.tensor_tensor(pT[1][:, :, :], T[0][:, :, :], pT[0][:, :, :].bitcast(F32),
                                          ALU.subtract).then_inc(T_free[0], 1)
                    if first and u == DU + 1:
                        dve.wait_ge(consts_ready, 3)
                        for part, value in ((later[:, :], masks[:, 0, :]), (ones[:, :], masks[:, 1, :]),
                                            (unseen[:, 0, :], masks[:, 2, :]), (unseen[:, 1, :], masks[:, 2, :]),
                                            (ident_r[:, :], ident[:, :])):
                            dve.tensor_copy(part, value).then_inc(parts_ready, 1)
                    if first and 1 <= u <= DU:
                        t, tb = (u - 1) // 2, (u - 1) % 2
                        for half in range(2):
                            dve.wait_ge(x_loaded[2 * t + half], 16)
                        dve.wait_ge(x_ssq_ready, u - 1)
                        part = x[:, tb, t * NT:(t + 1) * NT]
                        dve.tensor_tensor_reduce(junk[:, :], part, part, 1.0, 0.0, ALU.mult, ALU.add,
                                                 x_ssq[:, t, tb:tb + 1]).then_inc(x_ssq_ready, 1)
                    if not first:
                        if u == 1:
                            keep_v(g - 1)
                        attend(u, g - 1, A_EVERY)
                    for part, (to, gain) in enumerate(((qT, QG), (kT, KG))):
                        end = (part + 1) * DU - 1
                        if u == end + 3:
                            sum_heads(2 * g + part)
                        if u == end + 6:
                            norm_heads(2 * g + part, part, 4 * g + 2 * part)
                        if u == end + 8:
                            turn_heads(to, gain, 4 * g + 2 * part, 0)
                        if u == min(end + 10, AU - 1):
                            turn_heads(to, gain, 4 * g + 2 * part + 1, 1)

            dve.wait_ge(gains_turned, 1)
            dve.tensor_copy(gains[:, 0:KD], Z[:, 0:KD]).then_inc(gains_ready, 1)
            dve.wait_ge(gains_ready, 1)
            group(0, first=True)
            with nc.Fori(1, GROUPS, engines=[mybir.EngineType.DVE], hint_back_edge=True) as g:
                group(g)

            def add_residual(t, tile, U, pair, k, stores):
                dve.wait_ge(T_ready, SETS0 + 2 * k)
                dve.wait_ge(x_stored, stores)
                dve.wait_ge(x_ssq_ready, (stores + XN) * TB)
                for tb in range(TB):
                    if tb == 0:
                        dve.wait_ge(half_done, tile + 1)
                    else:
                        dve.wait_ge(unit_used, U + 1)
                    dve.tensor_tensor(stage[:, tb, :], acc[pair][tb][:, :], x[:, tb, bass.ts(t, NT)],
                                      ALU.add).then_inc(acc_free[pair][tb], 1)

            for u, (t, blocks) in enumerate(B_HEAD):
                lo(B0 + u, u, len(blocks))
                if u == 1:
                    keep_v(GROUPS - 1)
                attend(u, GROUPS - 1, B_EVERY)
            for u in range(DU):
                lo(B2 + u, u, 2)
                for t in range(2):
                    end = B_END[t] - BH
                    if u == end + 3:
                        add_residual(t, TBO + t, B2 + end, t, t, t)
                    if u == end + 6:
                        turn_tile(t, FFN, t)
            for u in range(DU):
                lo(B2 + DU + u, u, 2)
                if u == 1:
                    add_residual(2, TBO + 2, B2 + DU - 1, 0, 2, 2)
                if u == 5:
                    turn_tile(2, FFN, 2)

            def turn_hidden(j, k):
                for b in range(2):
                    dve.wait_ge(turned_hi, SETS0 + 2 * k + b + 1)
                    dve.tensor_tensor(hT[1][:, bass.ds(j * CB + 2 * b, 2), :], T[b][:, :, :],
                                      hT[0][:, bass.ds(j * CB + 2 * b, 2), :].bitcast(F32), ALU.subtract).then_inc(T_free[b], 1)

            def times_up(j, U):
                for tb in range(TB):
                    dve.wait_ge(acc_free[0][tb], C_P0 + j + 1)
                    if tb == 0:
                        dve.wait_ge(half_done, TC + 2 * j + 2)
                    else:
                        dve.wait_ge(unit_used, U + 1)
                    dve.tensor_tensor(stage[:, tb, :], stage[:, tb, :], acc[1][tb][:, :], ALU.mult).then_inc(acc_free[1][tb], 1)

            def gate_up(j, first=False):
                U0 = C0 + j * CU
                for u in range(CU):
                    lo(U0 + u, u, 2)
                    if u == 1:
                        if first:
                            add_residual(XN - 1, TBO + XN - 1, C0 - 1, 0, XN - 1, XN - 1)
                        else:
                            times_up(j - 1, U0 - 1)
                    if u == 5:
                        if first:
                            turn_tile(XN - 1, FFN, XN - 1)
                        else:
                            turn_hidden(j - 1, C_SET + j)
                    if u == DU + 2:
                        for tb in range(TB):
                            dve.wait_ge(sig_ready, TB * j + tb + 1)
                            dve.scalar_tensor_tensor(out=stage[:, tb, :], in0=acc[0][tb][:, :], scalar=rstd2[:, tb:tb + 1],
                                                     in1=stage[:, tb, :], op0=ALU.mult, op1=ALU.mult).then_inc(acc_free[0][tb], 1)

            gate_up(0, first=True)
            with nc.Fori(1, FN, engines=[mybir.EngineType.DVE], hint_back_edge=True) as j:
                gate_up(j)

            def down(n, first=False):
                for u in range(FU):
                    lo(D0 + n * FU + u, u, len(F_UNITS[u]))
                    if u == 1:
                        if first:
                            times_up(FN - 1, D0 - 1)
                        else:
                            add_residual(n - 1, TD + n - 1, D0 + n * FU - 1, 0, D_SET + n, XN + n - 1)
                    if u == 5:
                        if first:
                            turn_hidden(FN - 1, D_SET)
                        else:
                            turn_tile(n - 1, PLE, D_SET + n)

            down(0, first=True)
            with nc.Fori(1, XN, engines=[mybir.EngineType.DVE], hint_back_edge=True) as n:
                down(n)

            def add_embedding(n, U):
                for tb in range(TB):
                    dve.wait_ge(acc_free[0][tb], E_P0 + n + 1)
                    if tb == 0:
                        dve.wait_ge(half_done, TE + 2 * n + 2)
                    else:
                        dve.wait_ge(unit_used, U + 1)
                    dve.tensor_tensor(stage[:, tb, :], stage[:, tb, :], acc[1][tb][:, :], ALU.mult).then_inc(acc_free[1][tb], 1)
                    dve.wait_ge(acc_free[1][tb], E_P1 + n + 1)
                    part = x[:, tb, bass.ts(n, NT)]
                    dve.tensor_tensor(part, part, stage[:, tb, :], ALU.add).then_inc(x_final, 1)

            def embed(n, first=False):
                U0 = E0 + n * EU
                for u in range(EU):
                    lo(U0 + u, u, len(G_UNITS[u]) if u < EU - 1 else KP)
                    if u == 1:
                        if first:
                            add_residual(XN - 1, TD + XN - 1, E0 - 1, 0, E_SET, 2 * XN - 1)
                        else:
                            add_embedding(n - 1, U0 - 1)
                    if first and u == 5:
                        turn_tile(XN - 1, PLE, E_SET)

            embed(0, first=True)
            with nc.Fori(1, XN, engines=[mybir.EngineType.DVE], hint_back_edge=True) as n:
                embed(n)
            add_embedding(XN - 1, E0 + XN * EU - 1)

        @block.tensor
        def _(pe):
            TERMS = ((0, 0), (0, 1), (1, 0))

            def products(U, u, parts, blocks, pair, start, stop, before):
                pe.wait_ge(lo_ready, U + 1)
                for tb in range(TB):
                    if start:
                        pe.wait_ge(acc_free[pair][tb], before)
                    for i, c in enumerate(blocks):
                        for n, (a, w) in enumerate(TERMS):
                            last = pe.matmul(acc[pair][tb][:, :], parts[a][:, c, tb * P:(tb + 1) * P],
                                             w_parts[w][:, slot(u), i, :],
                                             start=(start and i == 0 and n == 0),
                                             stop=(stop and i == len(blocks) - 1 and n == 2))
                    if tb == TB - 1:
                        last.then_inc(unit_used, 1)
                    elif stop:
                        last.then_inc(half_done, 1)

            def turn(b, source, pairs, before):
                pe.wait_ge(T_free[b], before)
                for k in range(2):
                    for tb in range(TB):
                        last = pe.transpose(T[b][:, k, tb * P:(tb + 1) * P],
                                            source[:, tb, (pairs + k) * P:(pairs + k + 1) * P], ident[:, :])
                last.then_inc(T_ready, 1)

            def turn_stage(k, *stages):
                for pair, tiles in stages:
                    left(pe, pair, tiles)
                turn(0, stage, 0, SETS0_T0 + k)
                turn(1, stage, 2, SETS0_T1 + k)

            def three(out_ap, stationary, moving, start, stop):
                for n, (a, b) in enumerate(TERMS):
                    last = pe.matmul(out_ap, stationary[a], moving[b], start=(start and n == 0),
                                     stop=(stop and n == 2), skip_group_check=True)
                return last

            def scores(h, i, g):
                left_T0 = (X_ROUNDS + 1) // 2 + 4 * (g + 1)
                pe.wait_ge(T_free[0], left_T0)
                pe.wait_ge(z_free, h)
                q = [part[:, i, :] for part in qT]
                k = [part[:, i, :] for part in kT]
                own = Z[:, 0:3 * P].rearrange("p (b q) -> p b q", q=P)[:, 0:3:2, :]
                pe.matmul(own, ident_r[:, :], unseen[:, :, :], start=True, stop=False, skip_group_check=True)
                three(Z[:, 0:2 * P], [a[:, 0:P] for a in k], q, False, False)
                three(Z[:, 2 * P:3 * P], [a[:, P:2 * P] for a in k], [a[:, P:2 * P] for a in q],
                      False, True).then_inc(z_ready, 1)

            def rest(h, i):
                pe.wait_ge(neg_lo_ready, h + 1)
                pe.wait_ge(exponent_ready, h)
                for n, part in enumerate(neg_parts[i % 2]):
                    pe.matmul(R[:, 0:3 * P], later[:, :], part[:, :], start=(n == 0), stop=False)
                    last = pe.matmul(R[:, P:2 * P], ones[:, :], part[:, 2 * P:3 * P], start=False, stop=(n == 1))
                last.then_inc(rest_ready, 1)

            def weigh(h, i, g):
                pe.wait_ge(weight_lo_ready, h + 1)
                left(pe, 0, A_P0 + 2 * (g + 1))
                pe.wait_ge(oT_ready, h)
                w = weight_parts[i % 2]
                head = slice(i * HD, (i + 1) * HD)
                three(O[:, 0, :], [a[:, 0, head] for a in v], [a[:, 0:2 * P] for a in w], True, False)
                three(O[:, 0, P:2 * P], [a[:, 1, head] for a in v], [a[:, 2 * P:3 * P] for a in w],
                      False, True).then_inc(o_ready, 1)

            def attend(u, g, every):
                for h in range(HG):
                    if u == every * h + W_AT:
                        weigh(g * HG + h, h, g)
                    if u == every * h + R_AT:
                        rest(g * HG + h, h)
                    if u == every * h:
                        scores(g * HG + h, h, g)

            def turn_input(r):
                if r < KD // 2:
                    pe.wait_ge(x_loaded[r], 16)
                    turn(r % 2, x, 2 * r, r // 2)
                else:
                    pe.wait_ge(p_loaded, 16)
                    turn(0, p_sb, 0, r // 2)

            def group(g, first=False):
                U0 = A0 + g * AU
                for u in range(AU):
                    part, k = divmod(u, DU)
                    if first and u < DU:
                        if u == DU - 1:
                            rows = 2 * KD + 2
                            pe.wait_ge(gains_loaded, 16 * 4)
                            pe.wait_ge(gains_ready, 1)
                            pe.transpose(Z[:, KD:KD + rows], gain_rows[:, :], ident[0:rows, 0:rows]).then_inc(gains_turned, 1)
                        pe.wait_ge(T_free[u % 2], u // 2 + 1)
                        if u + 2 < X_ROUNDS:
                            turn_input(u + 2)
                    if not first:
                        attend(u, g - 1, A_EVERY)
                    for i in range(2):
                        for m in range(2):
                            if u == (i + 1) * DU + 4 + 2 * m:
                                left(pe, i, (A_P0 + 2 * g, A_P1 + g)[i] + 1)
                                turn(0, normed, 2 * m, (X_ROUNDS + 1) // 2 + 4 * g + 2 * i + m)
                    before = A_P1 + g if part == 1 else A_P0 + 2 * g + part // 2
                    products(U0 + u, u, xT, D_UNITS[k], part % 2, k == 0, k == DU - 1, before)

            pe.wait_ge(consts_ready, 1)
            def keep_busy(n):
                for _ in range(n):
                    pe.matmul(acc[0][0][:, 0:P], ident[:, :], ident[:, :], start=True, stop=True)

            keep_busy(WARM[0])
            pe.wait_ge(mix_loaded, 16)
            pe.transpose(Z[:, 0:KD], mix_rows[:, :], ident[0:KD, 0:KD]).then_inc(gains_turned, 1)
            turn_input(0)
            turn_input(1)
            keep_busy(WARM[1])
            group(0, first=True)
            pe.wait_ge(parts_ready, 5)
            with nc.Fori(1, GROUPS, engines=[mybir.EngineType.PE], hint_back_edge=True) as g:
                group(g)

            for u, (t, blocks) in enumerate(B_HEAD):
                attend(u, GROUPS - 1, B_EVERY)
                if blocks[-1] >= HEADS - HG:
                    pe.wait_ge(oT_ready, blocks[-1] + 1)
                products(B0 + u, u, oT, blocks, t, blocks[0] == 0, blocks[-1] == KD - 1, (B_P0, B_P1)[t])
            for n in range(XN - 2):
                for u in range(DU):
                    if n == 0 and u in (0, 2):
                        turn_stage(u // 2, B_LEFT[u // 2])
                    if n == 1 and u == 2:
                        turn_stage(2, B_LEFT[2])
                    products(B2 + n * DU + u, u, oT, D_UNITS[u], 0, u == 0, u == DU - 1, B_P0 + 1 + n)

            with nc.Fori(0, FN, engines=[mybir.EngineType.PE], hint_back_edge=True) as j:
                for u in range(CU):
                    part, k = divmod(u, DU)
                    if u == 2:
                        turn_stage(C_SET + j, (0, C_P0), (1, C_P1 + j))
                    if part == 0:
                        pe.wait_ge(T_free[k % 2], rounds_of_set(k // 2)[k % 2])
                    products(C0 + j * CU + u, u, xT, D_UNITS[k], part, k == 0, k == DU - 1, (C_P0, C_P1)[part] + j)

            with nc.Fori(0, XN, engines=[mybir.EngineType.PE], hint_back_edge=True) as n:
                for u in range(FU):
                    for b in range(2):
                        if u == 0:
                            pe.wait_ge(T_free[b], rounds_of_set(D_SET - 1)[b])
                        if F_UNITS[u][0] == KF - CB:
                            pe.wait_ge(T_free[b], rounds_of_set(D_SET)[b])
                    if u == 2:
                        turn_stage(D_SET + n, (1, E_P1), (0, D_P0 + n))
                    products(D0 + n * FU + u, u, hT, F_UNITS[u], 0, u == 0, u == FU - 1, D_P0 + n)

            def embed(n, first=False):
                for u in range(EU):
                    U = E0 + n * EU + u
                    if first and u == 2:
                        turn_stage(E_SET, (0, E_P0))
                    if u < EU - 1:
                        if first:
                            t, b = divmod(G_UNITS[u][-1] // 2, 2)
                            pe.wait_ge(T_free[b], rounds_of_set(D_SET + 1 + t)[b])
                        products(U, u, xT, G_UNITS[u], 0, u == 0, u == EU - 2, E_P0 + n)
                    else:
                        products(U, u, pT, list(range(KP)), 1, True, True, E_P1 + n)

            embed(0, first=True)
            with nc.Fori(1, XN, engines=[mybir.EngineType.PE], hint_back_edge=True) as n:
                embed(n)


_INS = ["x", "p", "norm_mix", "norm_ffn", "sb_w_in", "sb_q_gain", "sb_k_gain", "sb_w_out",
        "ffn_w_gate", "ffn_w_up", "ffn_w_down", "ple_norm", "ple_w_gate", "ple_w_proj"]
_FLAT = ("sb_w_in", "sb_w_out", "ffn_w_gate", "ffn_w_up", "ffn_w_down", "ple_w_gate", "ple_w_proj")


def kernel(**inputs):
    import concourse.bacc as bacc
    from concourse.bass_utils import run_bass_kernel_spmd

    nc = bacc.Bacc("TRN2", target_bir_lowering=False, num_devices=1)
    arrays, args = {}, []
    for name in _INS:
        a = np.ascontiguousarray(inputs[name])
        if name in _FLAT:
            a = a.reshape(a.shape[1:])
        arrays[f"in_{name}"] = a
        args.append(nc.dram_tensor(f"in_{name}", a.shape, mybir.dt.from_np(a.dtype), kind="ExternalInput").ap())
    out = nc.dram_tensor("out_0", inputs["x"].shape, F32, kind="ExternalOutput").ap()
    trunk(nc, *args, out)
    r = run_bass_kernel_spmd(nc, [arrays], core_ids=[0])
    return r.results[0]["out_0"]
```
